# Optimizing a Trainium2 kernel written in Bass

```python
import math
import jax, jax.numpy as jnp
from jax import lax
import numpy as np

D_MODEL = 1024
BATCH = 1
SEQ = 512
DEPTH = 2

N_META = 16
N_A = DEPTH // 2
N_B = DEPTH - N_A
HG_EXPAND = 128
HG_HEADS = D_MODEL // HG_EXPAND
HG_DK = HG_EXPAND
HG_DV = D_MODEL // HG_HEADS
HG_FDIM = HG_HEADS * HG_DK
HG_CHUNK = 64
F_FLOOR = 1e-30
DA_HEADS = D_MODEL // 128
DA_DH = 64
DA_DV = 2 * DA_DH
DA_QK = DA_HEADS * 2 * DA_DH
Q_BLOCK = 128
D_FF = ((8 * D_MODEL // 3) + 255) // 256 * 256
CONV_W = 3
EPS = 1e-5

kernel_name = "yoco_hgrn2_diffattn_convffn_meta"

def rmsnorm(x, g):
    xf = x.astype(jnp.float32)
    y = xf * lax.rsqrt(jnp.mean(xf * xf, axis=-1, keepdims=True) + EPS)
    return y.astype(x.dtype) * g

def hgrn2_lower_bounds(lb_param):
    p = jax.nn.softmax(lb_param.astype(jnp.float32), axis=0)
    return jnp.cumsum(p, axis=0) - p[0]

def gla_chunk_step(S, inp):
    q, k, v, lf = inp
    C = q.shape[2]
    tri = jnp.tril(jnp.ones((C, C), dtype=bool))
    b = jnp.cumsum(lf, axis=2)
    diff = b[:, :, :, None, :] - b[:, :, None, :, :]
    decay = jnp.exp(jnp.where(tri[None, None, :, :, None], diff, -jnp.inf))
    att = jnp.einsum('bhtd,bhsd,bhtsd->bhts', q, k, decay)
    o = jnp.einsum('bhts,bhse->bhte', att, v) + jnp.einsum('bhtd,bhde->bhte', q * jnp.exp(b), S)
    b_last = b[:, :, -1:, :]
    S = jnp.exp(b_last[:, :, 0, :, None]) * S + jnp.einsum('bhsd,bhse->bhde', k * jnp.exp(b_last - b), v)
    return S, o

def hgrn2_mixer(h, w_in, lb, gain_o, w_o):
    B, L, _ = h.shape
    f32 = jnp.float32
    proj = h @ w_in
    q, fz, i, g = jnp.split(proj, [HG_FDIM, 2 * HG_FDIM, 2 * HG_FDIM + D_MODEL], axis=-1)
    q = jax.nn.silu(q.astype(f32))
    fz = fz.astype(f32)
    lb = lb.astype(f32)
    sig = jax.nn.sigmoid(fz)
    f = lb + (1.0 - lb) * sig
    log_f = jnp.log(jnp.maximum(f, F_FLOOR))
    k = (1.0 - lb) * (1.0 - sig)
    v = i.astype(f32)
    pad = (-L) % HG_CHUNK
    n_chunks = (L + pad) // HG_CHUNK

    def to_chunks(t, d):
        t = jnp.pad(t.reshape(B, L, HG_HEADS, d), ((0, 0), (pad, 0), (0, 0), (0, 0)))
        return t.reshape(B, n_chunks, HG_CHUNK, HG_HEADS, d).transpose(1, 0, 3, 2, 4)

    xs = (to_chunks(q, HG_DK), to_chunks(k, HG_DK), to_chunks(v, HG_DV), to_chunks(log_f, HG_DK))
    S0 = jnp.zeros((B, HG_HEADS, HG_DK, HG_DV), f32)
    _, o = lax.scan(gla_chunk_step, S0, xs)
    o = o.transpose(1, 0, 3, 2, 4).reshape(B, n_chunks * HG_CHUNK, HG_HEADS, HG_DV)[:, pad:]
    o = o * lax.rsqrt(jnp.mean(o * o, axis=-1, keepdims=True) + EPS)
    o = o.reshape(B, L, D_MODEL) * gain_o.astype(f32) * jax.nn.silu(g.astype(f32))
    return o.astype(h.dtype) @ w_o

def shared_kv(h, kv_norm, w_kv):
    B, L, _ = h.shape
    pad = (-L) % Q_BLOCK
    kv = rmsnorm(h, kv_norm) @ w_kv
    k = kv[..., :DA_QK].reshape(B, L, DA_HEADS, 2, DA_DH)
    v = kv[..., DA_QK:].reshape(B, L, DA_HEADS, DA_DV)
    k = jnp.pad(k, ((0, 0), (0, pad), (0, 0), (0, 0), (0, 0)))
    v = jnp.pad(v, ((0, 0), (0, pad), (0, 0), (0, 0)))
    return k, v

def diff_attention(h, w_q, k_sh, v_sh, lam_q1, lam_k1, lam_q2, lam_k2, lam_init, sub_gain, w_o):
    B, L, _ = h.shape
    Lp = k_sh.shape[1]
    f32 = jnp.float32
    q = (h @ w_q).reshape(B, L, DA_HEADS, 2, DA_DH) * (DA_DH ** -0.5)
    q = jnp.pad(q, ((0, 0), (0, Lp - L), (0, 0), (0, 0), (0, 0)))
    lam = (jnp.exp(jnp.sum(lam_q1.astype(f32) * lam_k1.astype(f32)))
           - jnp.exp(jnp.sum(lam_q2.astype(f32) * lam_k2.astype(f32))) + lam_init)
    k_pos = jnp.arange(Lp)

    def block(i):
        qb = lax.dynamic_slice_in_dim(q, i * Q_BLOCK, Q_BLOCK, axis=1)
        s = jnp.einsum('bqhcd,bkhcd->bchqk', qb, k_sh).astype(f32)
        q_pos = i * Q_BLOCK + jnp.arange(Q_BLOCK)
        mask = q_pos[:, None] >= k_pos[None, :]
        p = jax.nn.softmax(jnp.where(mask, s, -jnp.inf), axis=-1)
        a = p[:, 0] - lam * p[:, 1]
        return jnp.einsum('bhqk,bkhe->bqhe', a.astype(v_sh.dtype), v_sh)

    o = lax.map(block, jnp.arange(Lp // Q_BLOCK))
    o = o.transpose(1, 0, 2, 3, 4).reshape(B, Lp, DA_HEADS, DA_DV)[:, :L].astype(f32)
    o = o * lax.rsqrt(jnp.mean(o * o, axis=-1, keepdims=True) + EPS) * sub_gain.astype(f32)
    o = o * (1.0 - lam_init)
    return o.reshape(B, L, D_MODEL).astype(h.dtype) @ w_o

def conv_ffn(h, w_up, conv_w, conv_b, w_down):
    u = h @ w_up
    u = lax.conv_general_dilated(u, conv_w[:, None, :], window_strides=(1,),
                                 padding=[(CONV_W - 1, 0)],
                                 dimension_numbers=('NWC', 'WIO', 'NWC'),
                                 feature_group_count=2 * D_FF) + conv_b
    a, b = jnp.split(u, 2, axis=-1)
    return (jax.nn.silu(a) * b) @ w_down

def setup_inputs(seed: int = 0) -> dict:
    key = jax.random.key(seed)
    ks = jax.random.split(key, 24)
    nrm = lambda k, shape, s: jax.random.normal(k, shape, jnp.float32) * s
    D = D_MODEL
    return {
        "x": nrm(ks[0], (BATCH, SEQ, D), 1.0),
        "meta_tokens": nrm(ks[1], (N_META, D), 1.0),
        "norm_mix": 1.0 + nrm(ks[2], (DEPTH, D), 0.02),
        "norm_ffn": 1.0 + nrm(ks[3], (DEPTH, D), 0.02),
        "hg_w_in": nrm(ks[4], (N_A, D, 2 * HG_FDIM + 2 * D), D ** -0.5),
        "hg_lb": nrm(ks[5], (N_A, HG_FDIM), 0.5),
        "hg_gain_o": 1.0 + nrm(ks[6], (N_A, D), 0.02),
        "hg_w_o": nrm(ks[7], (N_A, D, D), D ** -0.5),
        "kv_norm": 1.0 + nrm(ks[8], (D,), 0.02),
        "w_kv": nrm(ks[9], (D, DA_QK + DA_HEADS * DA_DV), D ** -0.5),
        "da_w_q": nrm(ks[10], (N_B, D, DA_QK), D ** -0.5),
        "da_lam_q1": nrm(ks[11], (N_B, DA_DH), 0.1),
        "da_lam_k1": nrm(ks[12], (N_B, DA_DH), 0.1),
        "da_lam_q2": nrm(ks[13], (N_B, DA_DH), 0.1),
        "da_lam_k2": nrm(ks[14], (N_B, DA_DH), 0.1),
        "da_sub_gain": 1.0 + nrm(ks[15], (N_B, DA_DV), 0.02),
        "da_w_o": nrm(ks[16], (N_B, D, D), D ** -0.5),
        "ffn_w_up": nrm(ks[17], (DEPTH, D, 2 * D_FF), D ** -0.5),
        "ffn_conv_w": nrm(ks[18], (DEPTH, CONV_W, 2 * D_FF), CONV_W ** -0.5),
        "ffn_conv_b": nrm(ks[19], (DEPTH, 2 * D_FF), 0.02),
        "ffn_w_down": nrm(ks[20], (DEPTH, D_FF, D), D_FF ** -0.5),
        "final_norm": 1.0 + nrm(ks[21], (D,), 0.02),
    }

def reference(x, meta_tokens, norm_mix, norm_ffn, hg_w_in, hg_lb, hg_gain_o, hg_w_o,
              kv_norm, w_kv, da_w_q, da_lam_q1, da_lam_k1, da_lam_q2, da_lam_k2,
              da_sub_gain, da_w_o, ffn_w_up, ffn_conv_w, ffn_conv_b, ffn_w_down, final_norm):
    B = x.shape[0]
    meta = jnp.broadcast_to(meta_tokens[None].astype(x.dtype), (B, N_META, D_MODEL))
    h = jnp.concatenate([meta, x], axis=1)
    lbs = hgrn2_lower_bounds(hg_lb)
    k_sh, v_sh = None, None
    for l in range(DEPTH):
        hn = rmsnorm(h, norm_mix[l])
        if l < N_A:
            h = h + hgrn2_mixer(hn, hg_w_in[l], lbs[l], hg_gain_o[l], hg_w_o[l])
        else:
            j = l - N_A
            lam_init = 0.8 - 0.6 * math.exp(-0.3 * l)
            h = h + diff_attention(hn, da_w_q[j], k_sh, v_sh, da_lam_q1[j], da_lam_k1[j],
                                   da_lam_q2[j], da_lam_k2[j], lam_init, da_sub_gain[j], da_w_o[j])
        h = h + conv_ffn(rmsnorm(h, norm_ffn[l]), ffn_w_up[l], ffn_conv_w[l], ffn_conv_b[l], ffn_w_down[l])
        if l == N_A - 1:
            k_sh, v_sh = shared_kv(h, kv_norm, w_kv)
    return rmsnorm(h, final_norm)[:, N_META:]


_drawn_inputs = setup_inputs


def setup_inputs(seed=0):
    import zlib

    import numpy as np

    out = dict(_drawn_inputs(seed))
    spreads = {}
    factors = {'norm_ffn': 2.932,
     'hg_gain_o': 3.782,
     'kv_norm': 4.062,
     'da_lam_k2': 3.019,
     'da_sub_gain': 26.827,
     'final_norm': 7.547,
     'ffn_conv_b': 2.76}
    for name, (base, spread) in spreads.items():
        noise = np.random.default_rng([zlib.crc32(name.encode()), seed]).standard_normal(out[name].shape)
        drawn = base * np.exp(spread * noise) if base else spread * noise
        out[name] = __import__('jax').numpy.asarray(drawn.astype(out[name].dtype))
    for name, factor in factors.items():
        out[name] = (out[name] * factor).astype(out[name].dtype)
    return out
```

```python
import math
from contextlib import ExitStack

import concourse.bass as bass
from concourse import mybir

F32 = mybir.dt.float32
F32R = mybir.dt.float32r
BF16 = mybir.dt.bfloat16
U8 = mybir.dt.uint8
ALU = mybir.AluOpType
ACT = mybir.ActivationFunctionType
AX_X = mybir.AxisListType.X

P = 128
D = 1024
KT = D // P
SEQ = 512
META = 16
T = SEQ + META
TH = T // 2
HEADS = D // P
D_FF = 2816
FT = D_FF // P
FB = 3
NC = SEQ // P
EPS = 1e-5
F_FLOOR = 1e-30
LN_SPLIT = 2.0 ** -60
MASKED = -1e30
LAM_INIT = 0.8 - 0.6 * math.exp(-0.3)
DH = 64
Q_SCALE = DH ** -0.5

STREAM = [("in", 4 * HEADS, 4 * HEADS), ("o_a", KT, KT), ("up_a", 2 * FT, 2 * FT), ("down_a", FB * KT, KT),
          ("kvq", 3 * HEADS, 3 * HEADS), ("o_b", KT, KT), ("up_b", 2 * FT, 2 * FT), ("down_b", FB * KT, KT)]
BLOCK0, OUT0 = {}, {}
_b = _o = 0
for _name, _nb, _no in STREAM:
    BLOCK0[_name], OUT0[_name] = _b, _o
    _b, _o = _b + _nb, _o + _no
NBLOCKS, NOUTS = _b, _o

VEC = {}
_c = 0
for _name, _w in [("norm_mix_a", KT), ("norm_mix_b", KT), ("norm_ffn_a", KT), ("norm_ffn_b", KT), ("lb", KT),
                  ("gain_o", KT), ("kv_norm", KT), ("final_norm", KT), ("sub_gain", 1), ("lam", 4),
                  ("conv_w_a", 3 * 2 * FT), ("conv_w_b", 3 * 2 * FT), ("conv_b_a", 2 * FT), ("conv_b_b", 2 * FT)]:
    VEC[_name] = _c
    _c += _w
NVEC = _c

LEVELS = [64, 32, 16, 8, 4, 2]
MASKED_LEVELS = [16, 8, 4, 2, 1]


def build(nc, wstream, xT, metaT, vecs, consts, out):
    address = [(nc.sbuf_base + 63) // 64 * 64]

    def place(name, shape, dt=F32, at=address):
        size = mybir.dt.size(dt)
        for s in shape[1:]:
            size *= s
        t = nc.alloc_sbuf_tensor_at(name, shape, dt, offset=at[0])
        at[0] += (size + 31) // 32 * 32
        return t

    ctx = ExitStack()
    with ctx:
        def sem(name):
            return ctx.enter_context(nc.semaphore(name))

        h = place("h", [P, KT, T])
        x_hi = place("x_hi", [P, KT, T], F32R)
        x_lo = place("x_lo", [P, KT, T], F32R)
        w_raw = place("w_raw", [P, 2, KT * P])
        w_hi = place("w_hi", [P, 2, KT * P], F32R)
        w_lo = place("w_lo", [P, 2, KT * P], F32R)
        rstd = place("rstd", [P, T])
        lntmp = place("lntmp", [P, T])
        sqb = place("sqb", [P, 2, T])
        sqsum = place("sqsum", [P, T])
        vec = place("vec", [P, NVEC])
        cst = place("cst", [P, 2 * P + T])
        msk_f = place("msk_f", [P, len(MASKED_LEVELS), P])
        msk = place("msk", [P, len(MASKED_LEVELS), P], U8)
        ones = place("ones", [P, P])
        ident_b = place("ident_b", [P, P], BF16)
        causal_b = place("causal_b", [P, P], BF16)
        small = place("small", [P, 64])
        ident, causal, chunk_keep = cst[:, 0:P], cst[:, P:2 * P], cst[:, 2 * P:2 * P + T]
        eps_c, nlam, sub_c, nlr = (small[:, i:i + 1] for i in range(4))
        carry, zero_c = small[:, 60:61], small[:, 61:62]
        lb_c, oml_c, noml_c, tmp_c, tmp2_c = (small[:, 8 * i:8 * i + 8] for i in range(1, 6))
        lamv, lame = small[0:DH, 48:50], small[:, 50:52]
        nmax, esum, rsum = small[:, 52:54], small[:, 54:56], small[:, 56:58]

        f_at = address[0]
        ub = [place(f"ub{j}", [P, T + 8]) for j in range(2)]
        cb = [place(f"cb{j}", [P, T]) for j in range(2)]
        sa = place("sa", [P, T])
        am = place("am", [P, T])
        f_end = address[0]
        at = [f_at]
        att = place("att", [P, NC, P], at=at)
        v_t = place("v_t", [P, NC, P], at=at)
        k_t = place("k_t", [P, NC - 1, P], at=at)
        state = place("state", [P, NC, P], at=at)
        k_meta_t = place("k_meta_t", [META, P], at=at)
        v_meta_t = place("v_meta_t", [META, P], at=at)
        att_meta = place("att_meta", [META, META], at=at)
        dec = place("dec", [P, 8], at=at)
        assert at[0] <= f_end
        at = [f_at]
        prob = [place(f"prob{c}", [P, T], at=at) for c in range(2)]
        attn = place("attn", [P, T], at=at)
        o_att = [place("o_att0", [P, T], at=at)]
        rs_att = place("rs_att", [P, T], at=at)
        attn_mt = place("attn_mt", [META, P], at=at)
        v_meta_h = place("v_meta_h", [META, P], at=at)
        assert at[0] <= f_end

        r_at = address[0]
        act_hi = place("act_hi", [P, FT, T], F32R)
        act_lo = place("act_lo", [P, FT, T], F32R)
        r_end = address[0]
        assert r_end <= nc.sbuf_usable_end, r_end
        at = [r_at]
        y_hi = place("y_hi", [P, KT, T], F32R, at=at)
        y_lo = place("y_lo", [P, KT, T], F32R, at=at)
        mixer_at = at[0]
        oo = place("oo", [P, KT, T], at=at)
        zf, zq, zv = (place(f"z{n}", [P, T], at=at) for n in "fqv")
        kk = place("kk", [P, T], at=at)
        qq = place("qq", [P, T], at=at)
        lf = place("lf", [P, T], at=at)
        lf2 = place("lf2", [P, T], at=at)
        fg = place("fg", [P, T], at=at)
        bb = place("bb", [P, T], at=at)
        qe = place("qe", [P, T], at=at)
        ks = place("ks", [P, T], at=at)
        lev = place("lev", [P, len(LEVELS), T], at=at)
        osq = place("osq", [P, T], at=at)
        rs = place("rs", [P, T], at=at)
        zg, sig_g = (zf, zq, zv), (fg, lf, lf2)
        assert at[0] <= r_end, (at[0], r_end)
        at = [mixer_at]
        xq_hi = place("xq_hi", [P, KT, T], F32R, at=at)
        xq_lo = place("xq_lo", [P, KT, T], F32R, at=at)
        kh = [place(f"kh{j}", [P, T], at=at) for j in range(2)]
        qh = [place(f"qh{j}", [P, T], at=at) for j in range(2)]
        zva = place("zva", [P, T], at=at)
        v_h = place("v_h", [P, NC, P], at=at)
        attn_t = place("attn_t", [P, NC, P], at=at)
        osq_att = place("osq_att", [P, T], at=at)
        o_att.append(place("o_att1", [P, T], at=at))
        assert at[0] <= r_end, (at[0], r_end)

        prod = ctx.enter_context(nc.psum_tensor("prod", [P, 2, 2, 512], F32))
        mix = ctx.enter_context(nc.psum_tensor("mix", [P, 4, 512], F32))

        def halves(t):
            return t.rearrange("p (a b) -> p a b", a=2)

        def out_ps(s):
            return prod[:, s, :, 0:TH]

        def main(t):
            return t[:, META:T]

        def blocks(t, c):
            return (t[:, 0:T] if c <= 8 else main(t)).rearrange("p (n w) -> p n w", w=2 * c)

        h_loaded = [sem(f"h_loaded{k}") for k in range(KT)]
        vec_loaded, meta_loaded, consts_loaded, stored = (
            sem(n) for n in ("vec_loaded", "meta_loaded", "consts_loaded", "stored"))
        raw_in = [sem(f"raw_in{s}") for s in range(2)]
        hi_ready, lo_ready, block_done, drained = sem("hi_ready"), sem("lo_ready"), sem("block_done"), sem("drained")
        ones_set, att_zero = sem("ones_set"), sem("att_zero")
        bf_ready, lb_step, lb_exp, lam_prod, lam_sum, lam_exp, lam_step = (
            sem(n) for n in ("bf_ready", "lb_step", "lb_exp", "lam_prod", "lam_sum", "lam_exp", "lam_step"))
        x_hi_done, x_ready, sq_done, sq_added, ms_done, ln_done, rstd_ready = (
            sem(n) for n in ("x_hi_done", "x_ready", "sq_done", "sq_added", "ms_done", "ln_done", "rstd_ready"))
        sig_done, f_done, k_done, clip_done, lnf_done, q_done, lf_done, b_done = (
            sem(n) for n in ("sig_done", "f_done", "k_done", "clip_done", "lnf_done", "q_done", "lf_done", "b_done"))
        qe_exp, ks_exp, dec_done, qe_done, ks_done, sub_done, lev_exp, lev_done, one_exp, one_done = (
            sem(n) for n in ("qe_exp", "ks_exp", "dec_done", "qe_done", "ks_done", "sub_done", "lev_exp", "lev_done",
                             "one_exp", "one_done"))
        vt_done, vt_copied, kt_done, kt_copied, u_done, s_done = (
            sem(n) for n in ("vt_done", "vt_copied", "kt_done", "kt_copied", "u_done", "s_done"))
        lp_done, lp_copied, lp_taken, lm_done, lm_taken = (
            sem(n) for n in ("lp_done", "lp_copied", "lp_taken", "lm_done", "lm_taken"))
        o_done, o_copied, osq_done, os_done, os_ln, rs_done, gate_done, y1_done, y2_done, y_hi_done, y_ready = (
            sem(n) for n in ("o_done", "o_copied", "osq_done", "os_done", "os_ln", "rs_done", "gate_done", "y1_done",
                             "y2_done", "y_hi_done", "y_ready"))
        base_done, tap_done, conv_done, silu_done, am_done, act_hi_done, act_ready = (
            sem(n) for n in ("base_done", "tap_done", "conv_done", "silu_done", "am_done", "act_hi_done", "act_ready"))
        pad_zero, mask_ready = sem("pad_zero"), sem("mask_ready")
        xq_hi_done, xq_ready, s_up, max_done, exp_done, rec_done, scaled, comb_done = (
            sem(n) for n in ("xq_hi_done", "xq_ready", "s_up", "max_done", "exp_done", "rec_done", "scaled", "comb_done"))
        at_done, at_copied, pv_done, pv_copied, va_done, va_copied = (
            sem(n) for n in ("at_done", "at_copied", "pv_done", "pv_copied", "va_done", "va_copied"))
        ao_sq, ao_sum, ao_ln, ao_rs, ao_y = (sem(n) for n in ("ao_sq", "ao_sum", "ao_ln", "ao_rs", "ao_y"))
        out_ready = sem("out_ready")

        B_IN, B_OA, B_UA, B_DA, B_KVQ, B_OB, B_UB, B_DB = (BLOCK0[n] for n, _, _ in STREAM)
        O_IN, O_OA, O_UA, O_DA, O_KVQ, O_OB, O_UB, O_DB = (OUT0[n] for n, _, _ in STREAM)

        def need(eng, s, value):
            if not (isinstance(value, int) and value <= 0):
                eng.wait_ge(s, value)

        block = ctx.enter_context(nc.Block())

        @block.sync
        def _(sp):
            sp.dma_start(vec[:, :], vecs).then_inc(vec_loaded, 16)
            sp.dma_start(h[:, :, 0:META], metaT).then_inc(meta_loaded, 16)
            for k in range(KT):
                sp.dma_start(h[:, k, META:T], xT[:, k, :]).then_inc(h_loaded[k], 16)
                if k == 0:
                    sp.dma_start(w_raw[:, 0, :], wstream[0]).then_inc(raw_in[0], 16)
                if k == 5:
                    sp.dma_start(w_raw[:, 1, :], wstream[1]).then_inc(raw_in[1], 16)
            sp.dma_start(cst[:, :], consts[:, 0:2 * P + T]).then_inc(consts_loaded, 16)
            sp.dma_start(msk_f[:, :, :], consts[:, 2 * P + T:].rearrange("p (a b) -> p a b", b=P)).then_inc(consts_loaded, 16)
            with sp.Fori(1, NBLOCKS // 2) as m:
                for s in range(2):
                    sp.wait_ge(lo_ready, 2 * m + s - 1)
                    sp.dma_start(w_raw[:, s, :], wstream[2 * m + s]).then_inc(raw_in[s], 16)
            for k in range(KT):
                sp.wait_ge(out_ready, k + 1)
                sp.dma_start(out[k], h[:, k, META:T]).then_inc(stored, 16)
            sp.wait_ge(stored, 16 * KT)

        @block.gpsimd
        def _(pool):
            pool.memset(ones[:, :], 1.0).then_inc(ones_set, 1)
            pool.memset(eps_c, EPS).then_inc(ones_set, 1)
            pool.memset(zero_c, 0.0).then_inc(ones_set, 1)
            pool.memset(att[:, :, :], 0.0).then_inc(att_zero, 1)
            pool.memset(att_meta[:, :], 0.0).then_inc(att_zero, 1)

            def norm_add(n):
                for k in range(KT):
                    pool.wait_ge(sq_done, KT * n + k + 1)
                    if k == 0:
                        need(pool, ms_done, n)
                        pool.tensor_copy(sqsum[:, :], sqb[:, 0, :]).then_inc(sq_added, 1)
                    else:
                        pool.wait_ge(sq_added, KT * n + k)
                        pool.tensor_tensor(sqsum[:, :], sqsum[:, :], sqb[:, k % 2, :], ALU.add).then_inc(sq_added, 1)

            def level_subs(c):
                pool.wait_ge(b_done, c)
                need(pool, lm_done, c - 1)
                for i, w in enumerate(LEVELS):
                    b3, l3 = blocks(bb, w), blocks(lev[:, i, :], w)
                    ref = b3[:, :, w - 1:w].broadcast_to([P, b3.shape[1], w])
                    pool.tensor_tensor(l3[:, :, 0:w], ref, b3[:, :, 0:w], ALU.subtract)
                    pool.tensor_tensor(l3[:, :, w:2 * w], b3[:, :, w:2 * w], ref, ALU.subtract).then_inc(sub_done, 1)

            norm_add(0)
            level_subs(1)
            with pool.Fori(2, HEADS + 1) as c:
                level_subs(c)
            for n in range(1, 5):
                norm_add(n)

        @block.scalar
        def _(act):
            def split(m, s):
                act.wait_ge(raw_in[s], 16 * m + 16)
                need(act, block_done, 2 * m + s - 1)
                act.activation(w_hi[:, s, :], w_raw[:, s, :], ACT.Copy).then_inc(hi_ready, 1)

            def norm_tile(n, k, s, gain):
                need(act, sq_added, KT * n + k - 1)
                act.activation(x_hi[:, k, :], h[:, k, :], ACT.Copy,
                               scale=vec[:, bass.ds(VEC[gain] + k, 1)]).then_inc(x_hi_done, 1)
                act.activation(sqb[:, s, :], h[:, k, :], ACT.Square).then_inc(sq_done, 1)

            def norm_rstd(n, outs):
                act.wait_ge(ms_done, n + 1)
                need(act, rstd_ready, n)
                act.activation(halves(lntmp[:, :]), mix[:, 0:2, 0:TH], ACT.Ln, bias=eps_c, scale=1.0 / D).then_inc(ln_done, 1)
                act.wait_ge(ln_done, n + 1)
                need(act, drained, outs)
                act.activation(rstd[:, :], lntmp[:, :], ACT.Exp, scale=-0.5).then_inc(rstd_ready, 1)

            act.wait_ge(vec_loaded, 16)
            act.wait_ge(meta_loaded, 16)
            act.wait_ge(ones_set, 3)
            for k in range(KT):
                act.wait_ge(h_loaded[k], 16)
                norm_tile(0, k, k % 2, "norm_mix_a")
                if k == 0:
                    split(0, 0)
                if k == 5:
                    split(0, 1)
            act.preload_act_table_set("natural_log_exp_and_others")
            split(1, 0)
            norm_rstd(0, 0)
            act.wait_ge(consts_loaded, 32)
            act.activation(ident_b[:, :], ident, ACT.Copy).then_inc(bf_ready, 1)
            act.activation(causal_b[:, :], causal, ACT.Copy).then_inc(bf_ready, 1)
            act.wait_ge(lb_step, 1)
            act.activation(tmp_c, tmp_c, ACT.Exp).then_inc(lb_exp, 1)
            act.wait_ge(lam_sum, 1)
            act.activation(lame, mix[:, 2, 0:2], ACT.Exp).then_inc(lam_exp, 1)

            def gla_sigmoids(hd):
                act.wait_ge(drained, 3 * hd + 2)
                act.activation(zf[:, :], zf[:, :], ACT.Sigmoid).then_inc(sig_done, 1)
                need(act, kt_done, hd)
                act.activation(ks[:, :], zq[:, :], ACT.Sigmoid).then_inc(sig_done, 1)

            def gla_ln(c):
                act.wait_ge(clip_done, 2 * c)
                act.activation(lf[:, :], lf[:, :], ACT.Ln).then_inc(lnf_done, 1)
                act.activation(lf2[:, :], lf2[:, :], ACT.Ln, scale=1.0 / LN_SPLIT).then_inc(lnf_done, 1)

            def copy_vt(c):
                act.wait_ge(vt_done, c)
                act.activation(v_t[:, :, :], mix[:, 2, :].rearrange("p (a b) -> p a b", b=P), ACT.Copy)
                act.activation(v_meta_t[:, :], mix[0:META, 3, 0:P], ACT.Copy).then_inc(vt_copied, 1)

            def ks_exps(c):
                need(act, s_done, NC * (c - 1))
                act.wait_ge(b_done, c)
                act.activation(dec[:, 0:NC - 1], bb[:, META + P - 1:T - 1:P], ACT.Exp).then_inc(dec_done, 1)
                act.wait_ge(q_done, c)
                act.activation(ks[:, 0:META], bb[:, 0:META], ACT.Exp, bias=bb[:, META - 1:META], scale=-1.0)
                for j in range(NC - 1):
                    a = META + j * P
                    last = act.activation(ks[:, a:a + P], bb[:, a:a + P], ACT.Exp,
                                          bias=bb[:, a + P - 1:a + P], scale=-1.0)
                last.then_inc(ks_exp, 1)

            def qe_exps(c):
                need(act, o_done, c - 1)
                act.activation(main(qe), main(bb), ACT.Exp).then_inc(qe_exp, 1)

            def gla_level(c, i):
                nl = len(LEVELS)
                act.wait_ge(sub_done, nl * (c - 1) + i + 1)
                part = lev[:, i, :] if LEVELS[i] <= 8 else lev[:, i, META:T]
                act.activation(part, part, ACT.Exp).then_inc(lev_exp, 1)

            def gla_one(c):
                act.activation(lf2[:, 0:TH], lf[:, 1::2], ACT.Exp)
                act.activation(lf2[:, TH:T], lf[:, 1::2], ACT.Exp, scale=-1.0).then_inc(one_exp, 1)

            def copy_kt(c):
                act.wait_ge(kt_done, c)
                act.activation(k_t[:, :, :], mix[:, 2, 0:(NC - 1) * P].rearrange("p (a b) -> p a b", b=P), ACT.Copy)
                act.activation(k_meta_t[:, :], mix[0:META, 3, P:2 * P], ACT.Copy).then_inc(kt_copied, 1)

            def copy_level64(c):
                need(act, o_done, c - 1)
                act.wait_ge(lp_done, 7 * (c - 1) + 1)
                act.activation(att[0:64, :, 64:128], mix[0:64, 0, 0:NC * 64].rearrange("p (a b) -> p a b", b=64),
                               ACT.Copy).then_inc(lp_copied, 1)

            def copy_level32(c):
                act.wait_ge(lp_done, 7 * (c - 1) + 2)
                for a in (0, 64):
                    last = act.activation(att[a:a + 32, :, a + 32:a + 64],
                                          mix[a:a + 32, 1, 0:NC * 32].rearrange("p (a b) -> p a b", b=32), ACT.Copy)
                last.then_inc(lp_copied, 1)

            def out_copy(c):
                act.wait_ge(o_done, c)
                need(act, os_done, c - 1)
                act.activation(main(osq), mix[:, 2, :], ACT.Square)
                act.activation(osq[:, 0:META], mix[:, 3, 0:META], ACT.Square).then_inc(osq_done, 1)
                act.activation(oo[:, c - 1, META:T], mix[:, 2, :], ACT.Copy)
                act.activation(oo[:, c - 1, 0:META], mix[:, 3, 0:META], ACT.Copy).then_inc(o_copied, 1)

            def out_rstd(c):
                act.wait_ge(os_done, c)
                need(act, y1_done, c - 1)
                act.activation(halves(rs[:, :]), mix[:, 0:2, 0:TH], ACT.Ln, bias=eps_c, scale=1.0 / P).then_inc(os_ln, 1)
                act.wait_ge(os_ln, c)
                act.activation(rs[:, :], rs[:, :], ACT.Exp, scale=-0.5).then_inc(rs_done, 1)

            def gate_sigmoid(j):
                act.wait_ge(drained, 3 * HEADS + j + 1)
                if j < 3:
                    act.wait_ge(one_done, HEADS)
                need(act, y2_done, j - 2)
                act.activation(sig_g[j % 3][:, :], zg[j % 3][:, :], ACT.Sigmoid).then_inc(sig_done, 1)

            def out_hi(j):
                act.wait_ge(y2_done, j + 1)
                act.activation(y_hi[:, j, :], oo[:, j, :], ACT.Copy).then_inc(y_hi_done, 1)

            def head(hd, m, par, gla, fin, last=False):
                def nxt(j):
                    q = 3 * par + j + 2
                    split(m + q // 2, q % 2)
                if gla:
                    gla_ln(hd)
                    nxt(0)
                    gla_level(hd, 0)
                if fin:
                    out_copy(hd - 1)
                if gla:
                    gla_level(hd, 1)
                    qe_exps(hd)
                    ks_exps(hd)
                    gla_level(hd, 2)
                if fin:
                    out_rstd(hd - 1)
                if gla:
                    gla_level(hd, 3)
                    copy_vt(hd)
                    gla_level(hd, 4)
                    gla_level(hd, 5)
                if gla:
                    copy_level64(hd)
                    copy_level32(hd)
                nxt(1)
                if gla:
                    copy_kt(hd)
                    gla_one(hd)
                if last:
                    for j in range(2):
                        gate_sigmoid(j)
                else:
                    gla_sigmoids(hd)
                nxt(2)
                if not last:
                    act.preload_act_table_set("natural_log_exp_and_others")

            head(0, 0, 0, False, False)
            head(1, 0, 1, True, False)
            with act.Fori(1, HEADS // 2) as i:
                head(2 * i, 3 * i, 0, True, True)
                head(2 * i + 1, 3 * i, 1, True, True)
            head(HEADS, 3 * HEADS // 2, 0, True, True, True)
            gate_sigmoid(2)
            out_hi(0)
            out_hi(1)
            for j in range(3, HEADS):
                n = 3 * HEADS + j + 2
                if j == 3:
                    out_copy(HEADS)
                split(n // 2, n % 2)
                gate_sigmoid(j)
                out_hi(j - 1)
                if j == 4:
                    act.preload_act_table_set("natural_log_exp_and_others")
                    out_rstd(HEADS)
            out_hi(HEADS - 1)
            act.preload_act_table_set("natural_log_exp_and_others")

            def out_phase(b0, o0, per, n, gain):
                with act.Fori(0, KT // 2) as i:
                    for s in range(2):
                        for j in range(per):
                            q = per * s + j
                            split(b0 // 2 + per * i + (q + 2) // 2, q % 2)
                        act.wait_ge(drained, o0 + 2 * i + s + 1)
                        norm_tile(n, 2 * i + s, s, gain)

            def ffn_up(b0, o0, f, n):
                cw, cbias = VEC[f"conv_w_{'ab'[f]}"], VEC[f"conv_b_{'ab'[f]}"]

                def tail_hi(p):
                    act.wait_ge(am_done, FT * f + p + 1)
                    act.wait_ge(consts_loaded, 32)
                    act.activation(act_hi[:, p, :], am[:, :], ACT.Copy).then_inc(act_hi_done, 1)

                def pair(p, prev):
                    for j in range(2):
                        split(b0 // 2 + p + 1, j)
                        if j == 0 and not prev:
                            norm_rstd(n, o0)
                        ft = 2 * p + j
                        act.wait_ge(drained, o0 + ft + 1)
                        need(act, am_done, FT * f + p)
                        act.wait_ge(consts_loaded, 32)
                        act.activation(cb[j][:, :], ub[j][:, 2:T + 2], ACT.Identity, bias=vec[:, bass.ds(cbias + ft, 1)],
                                       scale=vec[:, bass.ds(cw + 2 * 2 * FT + ft, 1)]).then_inc(base_done, 1)
                        if j == 0:
                            if prev:
                                tail_hi(p - 1)
                        else:
                            act.wait_ge(conv_done, 2 * FT * f + 2 * p + 1)
                            act.activation(sa[:, :], cb[0][:, :], ACT.Silu).then_inc(silu_done, 1)

                pair(0, False)
                with act.Fori(1, FT) as p:
                    pair(p, True)
                tail_hi(FT - 1)

            out_phase(B_OA, O_OA, 1, 1, "norm_ffn_a")
            ffn_up(B_UA, O_UA, 0, 1)
            act.preload_act_table_set("natural_log_exp_and_others")
            out_phase(B_DA, O_DA, FB, 2, "kv_norm")

            norm_rstd(2, O_DA)

            def xq_part(k0, k1):
                for k in range(k0, k1):
                    act.activation(xq_hi[:, k, :], h[:, k, :], ACT.Copy,
                                   scale=vec[:, VEC["norm_mix_b"] + k:VEC["norm_mix_b"] + k + 1]).then_inc(xq_hi_done, 1)

            act.wait_ge(block_done, B_KVQ)
            xq_part(0, KT // 2)
            def soft_exp(g, ti, c):
                nq, n, _ = tile_shape(ti)
                act.wait_ge(max_done, 10 * g + 2 * ti + c + 1)
                need(act, comb_done, 5 * g + ti)
                src = mix[0:nq, 2 * c, 0:n] if n <= 512 else mix[0:nq, 2 * c:2 * c + 2, 0:TH]
                dst = prob[c][0:nq, 0:n] if n <= 512 else halves(prob[c][0:nq, :])
                act.activation(dst, src, ACT.Exp, bias=nmax[0:nq, c:c + 1],
                               accum_out=esum[0:nq, c:c + 1]).then_inc(exp_done, 1)

            def at_copy(g, ti):
                nq, _, _ = tile_shape(ti)
                act.wait_ge(at_done, 5 * g + ti + 1)
                need(act, pv_done, 5 * g + ti)
                if ti:
                    act.activation(attn_t[:, 0:ti, :], prod[:, 1, 0, 0:ti * P].rearrange("p (a b) -> p a b", b=P), ACT.Copy)
                act.activation(attn_mt[:, 0:nq], prod[0:META, 1, 1, 0:nq], ACT.Copy).then_inc(at_copied, 1)

            def pv_copy(g, ti, par):
                nq, _, q0 = tile_shape(ti)
                act.wait_ge(pv_done, 5 * g + ti + 1)
                if ti == 0:
                    need(act, y_ready, HEADS + g - 1)
                act.activation(o_att[par][:, q0:q0 + nq], prod[:, 1, 1, P:P + nq], ACT.Copy).then_inc(pv_copied, 1)

            def att_square(g, par):
                act.wait_ge(pv_copied, 5 * g + 5)
                need(act, ao_sum, g)
                act.activation(osq_att[:, :], o_att[par][:, :], ACT.Square).then_inc(ao_sq, 1)

            def att_rstd(g):
                act.wait_ge(ao_sum, g + 1)
                need(act, ao_y, g)
                for a in range(2):
                    last = act.activation(rs_att[:, a * TH:(a + 1) * TH], mix[:, 2 * a + 1, 0:TH], ACT.Ln, bias=eps_c,
                                          scale=1.0 / P)
                last.then_inc(ao_ln, 1)
                act.wait_ge(ao_ln, g + 1)
                act.activation(rs_att[:, :], rs_att[:, :], ACT.Exp, scale=-0.5).then_inc(ao_rs, 1)

            def att_hi(g, par):
                act.wait_ge(ao_y, g + 1)
                act.wait_ge(consts_loaded, 32)
                act.activation(y_hi[:, g, :], o_att[par][:, :], ACT.Copy).then_inc(y_hi_done, 1)

            def v_copy(hd):
                act.wait_ge(va_done, hd + 1)
                act.activation(v_h[:, :, :], prod[:, 1, 0, :].rearrange("p (a b) -> p a b", b=P), ACT.Copy)
                act.activation(v_meta_h[:, :], prod[0:META, 1, 1, 0:P], ACT.Copy).then_inc(va_copied, 1)

            def kvq(hd, m, par, blocks_too, attend, fin):
                def nxt(j):
                    if blocks_too:
                        q = 3 * par + j + 2
                        split(m + q // 2, q % 2)
                g, gp, gg = hd - 1, 1 - par, hd - 2
                if attend:
                    soft_exp(g, 0, 0)
                    soft_exp(g, 0, 1)
                if fin:
                    att_rstd(gg)
                if attend:
                    soft_exp(g, 1, 0)
                    soft_exp(g, 1, 1)
                if fin:
                    att_hi(gg, par)
                if attend:
                    at_copy(g, 0)
                    soft_exp(g, 2, 0)
                    pv_copy(g, 0, gp)
                    soft_exp(g, 2, 1)
                    at_copy(g, 1)
                nxt(0)
                if not attend:
                    xq_part(KT // 2, KT)
                if attend:
                    pv_copy(g, 1, gp)
                    soft_exp(g, 3, 0)
                    soft_exp(g, 3, 1)
                    at_copy(g, 2)
                    pv_copy(g, 2, gp)
                    soft_exp(g, 4, 0)
                    at_copy(g, 3)
                nxt(1)
                if attend:
                    soft_exp(g, 4, 1)
                    pv_copy(g, 3, gp)
                    at_copy(g, 4)
                    pv_copy(g, 4, gp)
                    att_square(g, gp)
                nxt(2)
                if blocks_too:
                    v_copy(hd)

            mb = B_KVQ // 2
            kvq(0, mb, 0, True, False, False)
            kvq(1, mb, 1, True, True, False)
            with act.Fori(1, HEADS // 2) as i:
                kvq(2 * i, mb + 3 * i, 0, True, True, True)
                kvq(2 * i + 1, mb + 3 * i, 1, True, True, True)
            kvq(HEADS, 0, 0, False, True, True)
            att_rstd(HEADS - 1)
            att_hi(HEADS - 1, 1)

            out_phase(B_OB, O_OB, 1, 3, "norm_ffn_b")
            ffn_up(B_UB, O_UB, 1, 3)
            act.preload_act_table_set("natural_log_exp_and_others")
            for m in range(KT):
                for j in range(FB):
                    q = FB * m + j + 2
                    if q < FB * KT:
                        split(B_DB // 2 + q // 2, q % 2)
                act.wait_ge(drained, O_DB + m + 1)
                act.wait_ge(sq_added, KT * 4 + m - 1)
                act.activation(sqb[:, m % 2, :], h[:, m, :], ACT.Square).then_inc(sq_done, 1)
            norm_rstd(4, NOUTS)

        @block.vector
        def _(dve):
            def split(m, s):
                dve.wait_ge(hi_ready, 2 * m + s + 1)
                dve.tensor_tensor(w_lo[:, s, :], w_raw[:, s, :], w_hi[:, s, :].bitcast(F32), ALU.subtract).then_inc(lo_ready, 1)

            def norm_tile(n, k, gain):
                dve.wait_ge(x_hi_done, KT * n + k + 1)
                dve.scalar_tensor_tensor(x_lo[:, k, :], h[:, k, :], vec[:, bass.ds(VEC[gain] + k, 1)],
                                         x_hi[:, k, :].bitcast(F32), ALU.mult, ALU.subtract).then_inc(x_ready, 1)

            def scaled_out(dst, s, block_no, scale=None):
                dve.wait_ge(block_done, block_no)
                if scale is None:
                    dve.tensor_tensor(halves(dst), out_ps(s), halves(rstd[:, :]), ALU.mult).then_inc(drained, 1)
                else:
                    dve.scalar_tensor_tensor(halves(dst), out_ps(s), scale, halves(rstd[:, :]),
                                             ALU.mult, ALU.mult).then_inc(drained, 1)

            dve.wait_ge(vec_loaded, 16)
            for k in range(KT):
                norm_tile(0, k, "norm_mix_a")
                if k == 0:
                    split(0, 0)
                if k == 5:
                    split(0, 1)
            lbp = vec[:, VEC["lb"]:VEC["lb"] + KT]
            dve.tensor_tensor(tmp_c, lbp, lbp, ALU.subtract).then_inc(lb_step, 1)
            v0 = VEC["lam"]
            dve.tensor_tensor(lamv, vec[0:DH, v0:v0 + 2], vec[0:DH, v0 + 2:v0 + 4], ALU.mult).then_inc(lam_prod, 1)
            dve.tensor_single_scalar(sub_c, vec[:, VEC["sub_gain"]:VEC["sub_gain"] + 1], 1.0 - LAM_INIT, ALU.mult)
            dve.wait_ge(consts_loaded, 32)
            dve.tensor_copy(msk[:, :, :], msk_f[:, :, :]).then_inc(mask_ready, 1)
            split(1, 0)
            dve.wait_ge(lb_exp, 1)
            dve.reciprocal(tmp2_c, tmp_c).then_inc(lb_step, 1)
            dve.wait_ge(lb_step, 2)
            dve.tensor_tensor(tmp_c, tmp_c, tmp2_c, ALU.mult).then_inc(lb_step, 1)
            dve.wait_ge(lb_step, 3)
            dve.tensor_tensor(lb_c, tmp_c, tmp_c, ALU.subtract).then_inc(lb_step, 1)
            dve.wait_ge(lb_step, 4)
            dve.tensor_scalar(oml_c, lb_c, -1.0, 1.0, ALU.mult, ALU.add).then_inc(lb_step, 1)
            dve.tensor_scalar(noml_c, lb_c, 1.0, -1.0, ALU.mult, ALU.add).then_inc(lb_step, 1)
            dve.wait_ge(lam_exp, 1)
            dve.tensor_tensor(nlam, lame[:, 1:2], lame[:, 0:1], ALU.subtract).then_inc(lam_step, 1)
            dve.wait_ge(lam_step, 1)
            dve.tensor_single_scalar(nlam, nlam, -LAM_INIT, ALU.add).then_inc(lam_step, 1)
            dve.wait_ge(rstd_ready, 1)

            def evac(hd, j, dst):
                b = 4 * hd + j + 1
                scaled_out(dst, j % 2, b)

            def gla_gates(c):
                g = c - 1
                need(dve, lm_done, g)
                dve.wait_ge(sig_done, 2 * g + 1)
                dve.tensor_scalar(fg[:, :], zf[:, :], oml_c[:, bass.ds(g, 1)], lb_c[:, bass.ds(g, 1)],
                                  ALU.mult, ALU.add).then_inc(f_done, 1)
                dve.tensor_scalar(kk[:, :], zf[:, :], noml_c[:, bass.ds(g, 1)], oml_c[:, bass.ds(g, 1)],
                                  ALU.mult, ALU.add).then_inc(k_done, 1)
                dve.wait_ge(f_done, c)
                dve.tensor_single_scalar(lf[:, :], fg[:, :], LN_SPLIT, ALU.max).then_inc(clip_done, 1)
                dve.tensor_scalar(lf2[:, :], fg[:, :], LN_SPLIT, F_FLOOR, ALU.min, ALU.max).then_inc(clip_done, 1)
                dve.wait_ge(sig_done, 2 * g + 2)
                dve.tensor_tensor(qq[:, :], zq[:, :], ks[:, :], ALU.mult).then_inc(q_done, 1)

            def decays(c):
                dve.wait_ge(lnf_done, 2 * c)
                dve.tensor_tensor(lf[:, :], lf[:, :], lf2[:, :], ALU.add).then_inc(lf_done, 1)
                dve.wait_ge(lf_done, c)
                dve.tensor_tensor_scan(bb[:, :], chunk_keep, lf[:, :], 0.0, ALU.mult, ALU.add).then_inc(b_done, 1)

            def level_mul(c, i):
                w = LEVELS[i]
                dve.wait_ge(lev_exp, len(LEVELS) * (c - 1) + i + 1)
                l3, k3, q3 = blocks(lev[:, i, :], w), blocks(kk, w), blocks(qq, w)
                dve.tensor_tensor(l3[:, :, 0:w], l3[:, :, 0:w], k3[:, :, 0:w], ALU.mult)
                dve.tensor_tensor(l3[:, :, w:2 * w], l3[:, :, w:2 * w], q3[:, :, w:2 * w], ALU.mult).then_inc(lev_done, 1)

            def ks_mul(c):
                dve.wait_ge(ks_exp, c)
                dve.tensor_tensor(ks[:, 0:T - P], ks[:, 0:T - P], kk[:, 0:T - P], ALU.mult).then_inc(ks_done, 1)

            def qe_mul(c):
                dve.wait_ge(qe_exp, c)
                dve.tensor_tensor(main(qe), main(qe), main(qq), ALU.mult).then_inc(qe_done, 1)

            def level_one(c):
                dve.wait_ge(one_exp, c)
                dve.wait_ge(lev_done, len(LEVELS) * c)
                dve.tensor_tensor(qq[:, 1::2], qq[:, 1::2], lf2[:, 0:TH], ALU.mult)
                dve.tensor_tensor(kk[:, 1::2], kk[:, 1::2], lf2[:, TH:T], ALU.mult).then_inc(one_done, 1)

            def take_level(c, i):
                dve.wait_ge(mask_ready, 1)
                if i == 0:
                    need(dve, o_done, c - 1)
                    need(dve, lm_taken, 4 * (c - 1))
                    dve.wait_ge(lp_copied, 2 * c)
                need(dve, lp_taken, 5 * (c - 1) + i)
                dve.wait_ge(lp_done, 7 * (c - 1) + 3 + i)
                dve.tensor_copy(carry, zero_c)
                m = msk[:, i:i + 1, :].broadcast_to([P, NC, P])
                dve.copy_predicated(att[:, :, :], m, mix[:, i % 2, :].rearrange("p (a b) -> p a b", b=P)).then_inc(lp_taken, 1)

            def take_meta(c):
                dve.wait_ge(lm_done, c)
                dve.wait_ge(lp_taken, 5 * c)
                for i in range(1, 5):
                    need(dve, lm_taken, 4 * (c - 1) + i - 1)
                    dve.tensor_copy(carry, zero_c)
                    dve.copy_predicated(att_meta[:, :], msk[0:META, i, 0:META],
                                        mix[0:META, 3, 2 * P + META * i:2 * P + META * (i + 1)]).then_inc(lm_taken, 1)

            def states(c):
                dve.wait_ge(u_done, c)
                dve.wait_ge(dec_done, c)
                need(dve, o_done, c - 1)
                dve.tensor_copy(state[:, 0, :], mix[:, 2, 0:P]).then_inc(s_done, 1)
                for j in range(1, NC):
                    dve.wait_ge(s_done, NC * (c - 1) + j)
                    dve.scalar_tensor_tensor(state[:, j, :], state[:, j - 1, :], dec[:, j - 1:j],
                                             mix[:, 2, j * P:(j + 1) * P], ALU.mult, ALU.add).then_inc(s_done, 1)

            def out_scale(c):
                dve.wait_ge(rs_done, c)
                dve.wait_ge(o_copied, c)
                dve.tensor_tensor(oo[:, c - 1, :], oo[:, c - 1, :], rs[:, :], ALU.mult).then_inc(y1_done, 1)

            def gate_out(j):
                z, sg = zg[j % 3], sig_g[j % 3]
                dve.wait_ge(sig_done, 2 * HEADS + j + 1)
                col = VEC["gain_o"] + j
                dve.scalar_tensor_tensor(sg[:, :], z[:, :], vec[:, col:col + 1], sg[:, :], ALU.mult, ALU.mult).then_inc(gate_done, 1)
                dve.wait_ge(gate_done, j + 1)
                dve.wait_ge(y1_done, j + 1)
                dve.tensor_tensor(oo[:, j, :], oo[:, j, :], sg[:, :], ALU.mult).then_inc(y2_done, 1)

            def out_lo(j):
                dve.wait_ge(y_hi_done, j + 1)
                dve.tensor_tensor(y_lo[:, j, :], oo[:, j, :], y_hi[:, j, :].bitcast(F32), ALU.subtract).then_inc(y_ready, 1)

            def head(hd, m, par, gla, fin):
                def nxt(j):
                    q = 3 * par + j + 2
                    split(m + q // 2, q % 2)
                def evac(j, dst):
                    scaled_out(dst, (3 * par + j) % 2, 3 * hd + j + 1)
                if gla:
                    gla_gates(hd)
                    decays(hd)
                    dve.wait_ge(k_done, hd)
                evac(0, zf[:, :])
                if gla:
                    nxt(0)
                    level_mul(hd, 0)
                    level_mul(hd, 1)
                    qe_mul(hd)
                    ks_mul(hd)
                    level_mul(hd, 2)
                if fin:
                    out_scale(hd - 1)
                if gla:
                    level_mul(hd, 3)
                evac(1, zq[:, :])
                if gla:
                    level_mul(hd, 4)
                    level_mul(hd, 5)
                    level_one(hd)
                nxt(1)
                if gla:
                    take_level(hd, 0)
                    take_level(hd, 1)
                    states(hd)
                    dve.wait_ge(vt_done, hd)
                evac(2, zv[:, :])
                if gla:
                    take_level(hd, 2)
                nxt(2)
                if gla:
                    take_level(hd, 3)
                    take_level(hd, 4)
                    take_meta(hd)

            dve.wait_ge(att_zero, 2)
            dve.wait_ge(ones_set, 3)
            dve.wait_ge(mask_ready, 1)
            dve.wait_ge(lb_step, 6)
            head(0, 0, 0, False, False)
            head(1, 0, 1, True, False)
            with dve.Fori(1, HEADS // 2) as i:
                head(2 * i, 3 * i, 0, True, True)
                head(2 * i + 1, 3 * i, 1, True, True)
            head(HEADS, 3 * HEADS // 2, 0, True, True)
            gate_out(0)
            gate_out(1)
            out_lo(0)
            out_lo(1)
            for j in range(3, HEADS):
                n = 3 * HEADS + j
                scaled_out(zg[j % 3][:, :], j % 2, n + 1)
                split((n + 2) // 2, n % 2)
                if j == 3:
                    gate_out(2)
                if j == 5:
                    out_scale(HEADS)
                if j > 3:
                    out_lo(j - 1)
                gate_out(j)
                if j == 3:
                    out_lo(2)
            out_lo(HEADS - 1)

            def out_phase(b0, o0, per, n, gain):
                with dve.Fori(0, KT // 2) as i:
                    for s in range(2):
                        for j in range(per):
                            q = per * s + j
                            if j == per - 1:
                                dve.wait_ge(block_done, b0 + 2 * per * i + q + 1)
                                hk = h[:, 2 * i + s, :]
                                dve.tensor_tensor(halves(hk), out_ps(s), halves(hk), ALU.add).then_inc(drained, 1)
                            split(b0 // 2 + per * i + (q + 2) // 2, q % 2)
                        norm_tile(n, 2 * i + s, gain)

            def ffn_up(b0, o0, f, n):
                cw = VEC[f"conv_w_{'ab'[f]}"]
                dve.wait_ge(rstd_ready, n + 1)

                def tail_lo(p):
                    dve.wait_ge(act_hi_done, FT * f + p + 1)
                    dve.tensor_tensor(act_lo[:, p, :], am[:, :], act_hi[:, p, :].bitcast(F32), ALU.subtract).then_inc(act_ready, 1)

                def pair(p, prev):
                    for j in range(2):
                        ft = 2 * p + j
                        cnt = 2 * FT * f + ft + 1
                        need(dve, base_done, cnt - 2)
                        need(dve, conv_done, cnt - 2)
                        scaled_out(ub[j][:, 2:T + 2], j, b0 + ft + 1)
                        split(b0 // 2 + p + 1, j)
                        dve.wait_ge(base_done, cnt)
                        dve.scalar_tensor_tensor(cb[j][:, :], ub[j][:, 1:T + 1], vec[:, bass.ds(cw + 2 * FT + ft, 1)],
                                                 cb[j][:, :], ALU.mult, ALU.add).then_inc(tap_done, 1)
                        dve.wait_ge(tap_done, cnt)
                        dve.scalar_tensor_tensor(cb[j][:, :], ub[j][:, 0:T], vec[:, bass.ds(cw + ft, 1)],
                                                 cb[j][:, :], ALU.mult, ALU.add).then_inc(conv_done, 1)
                        if j == 0:
                            if prev:
                                tail_lo(p - 1)
                        else:
                            need(dve, act_ready, FT * f + p)
                            dve.wait_ge(silu_done, FT * f + p + 1)
                            dve.wait_ge(conv_done, cnt)
                            dve.tensor_tensor(am[:, :], sa[:, :], cb[1][:, :], ALU.mult).then_inc(am_done, 1)

                pair(0, False)
                with dve.Fori(1, FT) as p:
                    pair(p, True)
                tail_lo(FT - 1)

            out_phase(B_OA, O_OA, 1, 1, "norm_ffn_a")
            for j in range(2):
                dve.memset(ub[j][:, 0:2], 0.0).then_inc(pad_zero, 1)
            dve.wait_ge(pad_zero, 2)
            ffn_up(B_UA, O_UA, 0, 1)
            out_phase(B_DA, O_DA, FB, 2, "kv_norm")

            def xq_part(k0, k1):
                for k in range(k0, k1):
                    dve.wait_ge(xq_hi_done, k + 1)
                    dve.scalar_tensor_tensor(xq_lo[:, k, :], h[:, k, :], vec[:, VEC["norm_mix_b"] + k:VEC["norm_mix_b"] + k + 1],
                                             xq_hi[:, k, :].bitcast(F32), ALU.mult, ALU.subtract).then_inc(xq_ready, 1)

            xq_part(0, KT // 2)
            dve.wait_ge(rstd_ready, 3)

            def soft_max(g, ti, c):
                nq, n, _ = tile_shape(ti)
                dve.wait_ge(s_up, 10 * g + 2 * ti + c + 1)
                if n <= 512:
                    dve.tensor_reduce(nmax[0:nq, c:c + 1], mix[0:nq, 2 * c, 0:n], AX_X, ALU.max, negate=True).then_inc(max_done, 1)
                else:
                    dve.tensor_reduce(nmax[0:nq, c:c + 1], mix[0:nq, 2 * c:2 * c + 2, 0:TH], mybir.AxisListType.XY, ALU.max,
                                      negate=True).then_inc(max_done, 1)

            def combine(g, ti):
                nq, n, _ = tile_shape(ti)
                cnt = 5 * g + ti + 1
                dve.wait_ge(exp_done, 2 * cnt)
                need(dve, comb_done, cnt - 1)
                dve.reciprocal(rsum[0:nq, :], esum[0:nq, :]).then_inc(rec_done, 1)
                dve.wait_ge(rec_done, 2 * cnt - 1)
                dve.tensor_tensor(nlr[0:nq, :], rsum[0:nq, 1:2], nlam[0:nq, :], ALU.mult).then_inc(rec_done, 1)
                need(dve, at_done, cnt - 1)
                dve.tensor_scalar(attn[0:nq, 0:n], prob[0][0:nq, 0:n], rsum[0:nq, 0:1], None, ALU.mult).then_inc(scaled, 1)
                dve.wait_ge(rec_done, 2 * cnt)
                dve.wait_ge(scaled, cnt)
                dve.scalar_tensor_tensor(attn[0:nq, 0:n], prob[1][0:nq, 0:n], nlr[0:nq, :], attn[0:nq, 0:n],
                                         ALU.mult, ALU.add).then_inc(comb_done, 1)

            def att_out(g, par):
                dve.wait_ge(ao_rs, g + 1)
                o = o_att[par][:, :]
                dve.scalar_tensor_tensor(o, o, sub_c, rs_att[:, :], ALU.mult, ALU.mult).then_inc(ao_y, 1)

            def att_lo(g, par):
                dve.wait_ge(y_hi_done, HEADS + g + 1)
                dve.tensor_tensor(y_lo[:, g, :], o_att[par][:, :], y_hi[:, g, :].bitcast(F32), ALU.subtract).then_inc(y_ready, 1)

            def kvq(hd, m, par, blocks_too, attend, fin):
                def nxt(j):
                    q = 3 * par + j + 2
                    split(m + q // 2, q % 2)
                g, gp, gg = hd - 1, 1 - par, hd - 2
                if attend:
                    soft_max(g, 0, 0)
                    soft_max(g, 0, 1)
                    soft_max(g, 1, 0)
                    combine(g, 0)
                    soft_max(g, 1, 1)
                if fin:
                    att_out(gg, par)
                if attend:
                    combine(g, 1)
                    soft_max(g, 2, 0)
                if fin:
                    att_lo(gg, par)
                if attend:
                    soft_max(g, 2, 1)
                if blocks_too:
                    scaled_out(kh[par][:, :], 0, B_KVQ + 3 * hd + 1)
                if attend:
                    combine(g, 2)
                if blocks_too:
                    nxt(0)
                if not attend:
                    xq_part(KT // 2, KT)
                if attend:
                    soft_max(g, 3, 0)
                    soft_max(g, 3, 1)
                    combine(g, 3)
                    soft_max(g, 4, 0)
                if blocks_too:
                    need(dve, va_done, hd)
                    scaled_out(zva[:, :], 0 if attend else 1, B_KVQ + 3 * hd + 2)
                    nxt(1)
                if attend:
                    soft_max(g, 4, 1)
                    combine(g, 4)
                if blocks_too:
                    scaled_out(qh[par][:, :], 0, B_KVQ + 3 * hd + 3, Q_SCALE)
                    nxt(2)

            mb = B_KVQ // 2
            kvq(0, mb, 0, True, False, False)
            kvq(1, mb, 1, True, True, False)
            with dve.Fori(1, HEADS // 2) as i:
                kvq(2 * i, mb + 3 * i, 0, True, True, True)
                kvq(2 * i + 1, mb + 3 * i, 1, True, True, True)
            kvq(HEADS, 0, 0, False, True, True)
            att_out(HEADS - 1, 1)
            att_lo(HEADS - 1, 1)

            out_phase(B_OB, O_OB, 1, 3, "norm_ffn_b")
            for j in range(2):
                dve.memset(ub[j][:, 0:2], 0.0).then_inc(pad_zero, 1)
            dve.wait_ge(pad_zero, 4)
            ffn_up(B_UB, O_UB, 1, 3)
            for m in range(KT):
                for j in range(FB):
                    q = FB * m + j + 2
                    if j == FB - 1:
                        dve.wait_ge(block_done, B_DB + q - 1)
                        dve.tensor_tensor(halves(h[:, m, :]), out_ps(m % 2), halves(h[:, m, :]), ALU.add).then_inc(drained, 1)
                    if q < FB * KT:
                        split(B_DB // 2 + q // 2, q % 2)
            dve.wait_ge(rstd_ready, 5)
            dve.wait_ge(drained, NOUTS)
            for k in range(KT):
                dve.scalar_tensor_tensor(h[:, k, META:T], h[:, k, META:T],
                                         vec[:, VEC["final_norm"] + k:VEC["final_norm"] + k + 1], rstd[:, META:T],
                                         ALU.mult, ALU.mult).then_inc(out_ready, 1)

        @block.tensor
        def _(pe):
            def tiles(w, s, first, last, hi, lo, ready, ks, j0=0):
                n = len(ks)
                for j, k in enumerate(ks):
                    if ready is not None:
                        pe.wait_ge(ready[0], ready[1] + k + 1)
                    c = slice((j0 + j) * P, (j0 + j + 1) * P)
                    for p, (wt, xt) in enumerate(((w_hi, hi), (w_hi, lo), (w_lo, hi))):
                        for a in range(2):
                            mm = pe.matmul(prod[:, s, a, 0:TH], wt[:, w, c], xt[:, k, a * TH:(a + 1) * TH],
                                           start=first and j == 0 and p == 0, stop=last and j == n - 1 and p == 2)
                return mm

            def product(m, w, o, s, hi=x_hi, lo=x_lo, ready=None, free=None, k0=0, k1=KT):
                if k0 == 0:
                    pe.wait_ge(lo_ready, 2 * m + w + 1)
                    need(pe, drained, o - 1 if free is None else free)
                mm = tiles(w, s, k0 == 0, k1 == KT, hi, lo, ready, range(k0, k1), k0)
                if k1 == KT:
                    mm.then_inc(block_done, 1)

            def norm_sum(n):
                pe.wait_ge(sq_added, KT * (n + 1))
                for a in range(2):
                    mm = pe.matmul(mix[:, a, 0:TH], ones[:, :], sqsum[:, a * TH:(a + 1) * TH], start=True, stop=True)
                mm.then_inc(ms_done, 1)

            def v_transpose(c):
                pe.wait_ge(drained, 3 * c)
                if isinstance(c, int) and c == 1:
                    pe.wait_ge(lam_exp, 1)
                    pe.wait_ge(bf_ready, 2)
                need(pe, o_copied, c - 1)
                for j in range(NC):
                    pe.transpose(mix[:, 2, j * P:(j + 1) * P], zv[:, META + j * P:META + (j + 1) * P], ident)
                pe.transpose(mix[0:META, 3, 0:P], zv[:, 0:META], ident).then_inc(vt_done, 1)

            def k_transpose(c):
                pe.wait_ge(ks_done, c)
                pe.wait_ge(vt_copied, c)
                for j in range(NC - 1):
                    pe.transpose(mix[:, 2, j * P:(j + 1) * P], ks[:, META + j * P:META + (j + 1) * P], ident)
                pe.transpose(mix[0:META, 3, P:2 * P], ks[:, 0:META], ident).then_inc(kt_done, 1)

            def updates(c):
                pe.wait_ge(kt_copied, c)
                pe.matmul(mix[:, 2, 0:P], k_meta_t[:, :], v_meta_t[:, :], start=True, stop=True)
                for j in range(NC - 1):
                    mm = pe.matmul(mix[:, 2, (j + 1) * P:(j + 2) * P], k_t[:, j, :], v_t[:, j, :], start=True, stop=True)
                mm.then_inc(u_done, 1)

            def level64(c):
                pe.wait_ge(lev_done, 6 * (c - 1) + 1)
                need(pe, rs_done, c - 1)
                for j in range(NC):
                    a = META + j * P
                    mm = pe.matmul(mix[0:64, 0, j * 64:(j + 1) * 64], lev[:, 0, a:a + 64], lev[:, 0, a + 64:a + P],
                                   start=True, stop=True)
                mm.then_inc(lp_done, 1)

            def level32(c):
                pe.wait_ge(lev_done, 6 * (c - 1) + 2)
                for r in (0, 64):
                    for j in range(NC):
                        a = META + j * P + r
                        mm = pe.matmul(mix[r:r + 32, 1, j * 32:(j + 1) * 32], lev[:, 1, a:a + 32], lev[:, 1, a + 32:a + 64],
                                       start=True, stop=True)
                mm.then_inc(lp_done, 1)

            def level_masked(c, i):
                if i < 4:
                    pe.wait_ge(lev_done, 6 * (c - 1) + 3 + i)
                    k, q = lev[:, 2 + i, :], lev[:, 2 + i, :]
                else:
                    pe.wait_ge(one_done, c)
                    k, q = kk[:, :], qq[:, :]
                if i < 2:
                    pe.wait_ge(lp_copied, 2 * (c - 1) + 1 + i)
                else:
                    pe.wait_ge(lp_taken, 5 * (c - 1) + i - 1)
                for j in range(NC):
                    a = META + j * P
                    mm = pe.matmul(mix[:, i % 2, j * P:(j + 1) * P], k[:, a:a + P], q[:, a:a + P], start=True, stop=True)
                mm.then_inc(lp_done, 1)

            def levels_meta(c):
                for i in range(1, 5):
                    k, q = (lev[:, 2 + i, :], lev[:, 2 + i, :]) if i < 4 else (kk[:, :], qq[:, :])
                    mm = pe.matmul(mix[0:META, 3, 2 * P + META * i:2 * P + META * (i + 1)], k[:, 0:META], q[:, 0:META],
                                   start=True, stop=True)
                mm.then_inc(lm_done, 1)

            def outputs(c):
                pe.wait_ge(lp_taken, 5 * c)
                pe.wait_ge(lm_taken, 4 * c)
                pe.wait_ge(s_done, NC * c)
                pe.wait_ge(qe_done, c)
                for j in range(NC):
                    a = META + j * P
                    pe.matmul(mix[:, 2, j * P:(j + 1) * P], v_t[:, j, :], att[:, j, :], start=True, stop=False)
                    pe.matmul(mix[:, 2, j * P:(j + 1) * P], state[:, j, :], qe[:, a:a + P], start=False, stop=True)
                pe.matmul(mix[:, 3, 0:META], v_meta_t[:, :], att_meta[:, :], start=True, stop=True).then_inc(o_done, 1)

            def out_sum(c):
                pe.wait_ge(osq_done, c)
                pe.wait_ge(lp_taken, 5 * c)
                for a in range(2):
                    mm = pe.matmul(mix[:, a, 0:TH], ones[:, :], osq[:, a * TH:(a + 1) * TH], start=True, stop=True)
                mm.then_inc(os_done, 1)

            def head(hd, m, par, gla, fin):
                def blk(j, k0, k1, ready=None):
                    q = 3 * par + j
                    product(m + q // 2, q % 2, 3 * hd + j, q % 2, ready=ready, k0=k0, k1=k1)
                if not gla:
                    blk(0, 0, KT, (x_ready, 0))
                    blk(1, 0, 4)
                    norm_sum(0)
                    pe.wait_ge(lam_prod, 1)
                    pe.matmul(mix[:, 2, 0:2], ones[0:DH, :], lamv, start=True, stop=True).then_inc(lam_sum, 1)
                    blk(1, 4, KT)
                    blk(2, 0, KT)
                    return
                blk(0, 0, KT)
                blk(1, 0, 2)
                if fin:
                    outputs(hd - 1)
                blk(1, 2, 6)
                if fin:
                    out_sum(hd - 1)
                v_transpose(hd)
                blk(1, 6, KT)
                blk(2, 0, 1)
                level64(hd)
                level32(hd)
                blk(2, 1, 3)
                level_masked(hd, 0)
                k_transpose(hd)
                blk(2, 3, 4)
                level_masked(hd, 1)
                blk(2, 4, 6)
                updates(hd)
                blk(2, 6, KT)
                for i in (2, 3, 4):
                    level_masked(hd, i)
                levels_meta(hd)

            pe.wait_ge(ones_set, 3)
            head(0, 0, 0, False, False)
            pe.wait_ge(rstd_ready, 1)
            head(1, 0, 1, True, False)
            with pe.Fori(1, HEADS // 2) as i:
                head(2 * i, 3 * i, 0, True, True)
                head(2 * i + 1, 3 * i, 1, True, True)
            head(HEADS, 3 * HEADS // 2, 0, True, True)
            for j in range(3, HEADS):
                n = 3 * HEADS + j
                product(n // 2, n % 2, n, n % 2)
                if j == 3:
                    outputs(HEADS)
                if j == 4:
                    out_sum(HEADS)

            def out_model(b0, o0, y0, first=0):
                with pe.Fori(first, KT // 2) as i:
                    for s in range(2):
                        product(b0 // 2 + i, s, o0 + 2 * i + s, s, y_hi, y_lo, (y_ready, y0))

            def ffn_up(b0, o0, n):
                for s in range(2):
                    product(b0 // 2, s, o0 + s, s, ready=(x_ready, KT * n) if s == 0 else None)
                    if s == 0:
                        norm_sum(n)
                with pe.Fori(1, FT) as p:
                    for s in range(2):
                        product(b0 // 2 + p, s, o0 + 2 * p + s, s)

            def ffn_down(b0, o0, f):
                with pe.Fori(0, KT // 2) as i:
                    for s in range(2):
                        for j in range(FB):
                            q = FB * s + j
                            pe.wait_ge(lo_ready, b0 + 2 * FB * i + q + 1)
                            if j == 0:
                                pe.wait_ge(drained, o0 + 2 * i + s - 1)
                            tiles(q % 2, s, j == 0, j == FB - 1, act_hi, act_lo, (act_ready, FT * f),
                                  range(KT * j, min(KT * (j + 1), FT))).then_inc(block_done, 1)

            out_model(B_OA, O_OA, 0)
            pe.wait_ge(rs_done, HEADS)
            ffn_up(B_UA, O_UA, 1)
            ffn_down(B_DA, O_DA, 0)

            def scores(g, ti, c, par):
                nq, n, q0 = tile_shape(ti)
                u = 2 * ti + c
                if u == 0:
                    pe.wait_ge(drained, O_KVQ + 3 * g + 3)
                need(pe, exp_done, 10 * g + u - 1)
                r = slice(c * DH, (c + 1) * DH)
                if ti == 0:
                    pe.matmul(mix[0:nq, 2 * c, 0:n], ident_b[:, 0:nq], causal_b[:, 0:n], start=True, stop=False)
                    pe.matmul(mix[0:nq, 2 * c, 0:n], qh[par][r, 0:nq], kh[par][r, 0:n], start=False,
                              stop=True).then_inc(s_up, 1)
                    return
                for bank, (a, b) in enumerate(((0, n),) if n <= 512 else ((0, TH), (TH, T))):
                    has = b == n
                    mm = pe.matmul(mix[0:nq, 2 * c + bank, 0:b - a], qh[par][r, q0:q0 + nq], kh[par][r, a:b],
                                   start=True, stop=not has)
                    if has:
                        mm = pe.matmul(mix[:, 2 * c + bank, b - a - P:b - a], ident_b[:, :], causal_b[:, :],
                                       start=False, stop=True)
                mm.then_inc(s_up, 1)

            def a_transpose(g, ti):
                nq, n, _ = tile_shape(ti)
                need(pe, pv_copied, 5 * g + ti)
                if ti == 0:
                    pe.wait_ge(va_copied, g + 1)
                pe.wait_ge(comb_done, 5 * g + ti + 1)
                if ti == 0:
                    pe.matmul(prod[0:META, 1, 1, 256:256 + META], ident_b[:, 0:META], ident_b[:, 0:META],
                              start=True, stop=True)
                for j in range(ti):
                    pe.transpose(prod[:, 1, 0, j * P:(j + 1) * P], attn[:, META + j * P:META + (j + 1) * P], ident)
                pe.transpose(prod[0:META, 1, 1, 0:nq], attn[0:nq, 0:META], ident[0:nq, 0:nq]).then_inc(at_done, 1)

            def attend_v(g, ti):
                nq, n, _ = tile_shape(ti)
                pe.wait_ge(at_copied, 5 * g + ti + 1)
                o = prod[:, 1, 1, P:P + nq]
                mm = pe.matmul(o, v_meta_h[:, :], attn_mt[:, 0:nq], start=True, stop=ti == 0)
                for j in range(ti):
                    mm = pe.matmul(o, v_h[:, j, :], attn_t[:, j, :], start=False, stop=j == ti - 1)
                mm.then_inc(pv_done, 1)

            def att_sum(g):
                pe.wait_ge(ao_sq, g + 1)
                pe.wait_ge(exp_done, 10 * g + 10)
                for a in range(2):
                    mm = pe.matmul(mix[:, 2 * a + 1, 0:TH], ones[:, :], osq_att[:, a * TH:(a + 1) * TH], start=True, stop=True)
                mm.then_inc(ao_sum, 1)

            def va_transpose(hd):
                pe.wait_ge(drained, O_KVQ + 3 * hd + 2)
                for j in range(NC):
                    pe.transpose(prod[:, 1, 0, j * P:(j + 1) * P], zva[:, META + j * P:META + (j + 1) * P], ident)
                need(pe, pv_copied, 5 * hd)
                pe.transpose(prod[0:META, 1, 1, 0:P], zva[:, 0:META], ident).then_inc(va_done, 1)

            def kvq(hd, m, par, attend, fin):
                def blk(j, k0, k1):
                    q = 3 * par + j
                    o = O_KVQ + 3 * hd + j
                    hi, lo = (xq_hi, xq_lo) if j == 2 else (x_hi, x_lo)
                    ready = None if attend else ((x_ready, 2 * KT), None, (xq_ready, 0))[j]
                    s = 0 if attend else j % 2
                    product(m + q // 2, q % 2, o, s, hi, lo, ready, o if attend else o - 1, k0, k1)
                g, gp = hd - 1, 1 - par
                if not attend:
                    blk(0, 0, 5)
                    norm_sum(2)
                    blk(0, 5, KT)
                    blk(1, 0, KT)
                    blk(2, 0, KT)
                    va_transpose(hd)
                    return
                scores(g, 0, 0, gp)
                scores(g, 0, 1, gp)
                blk(0, 0, 1)
                if fin:
                    att_sum(g - 1)
                blk(0, 1, 2)
                scores(g, 1, 0, gp)
                scores(g, 1, 1, gp)
                blk(0, 2, 4)
                a_transpose(g, 0)
                blk(0, 4, 5)
                scores(g, 2, 0, gp)
                attend_v(g, 0)
                blk(0, 5, 6)
                scores(g, 2, 1, gp)
                blk(0, 6, 7)
                a_transpose(g, 1)
                blk(0, 7, KT)
                scores(g, 3, 0, gp)
                attend_v(g, 1)
                blk(1, 0, 2)
                scores(g, 3, 1, gp)
                blk(1, 2, 3)
                a_transpose(g, 2)
                blk(1, 3, 4)
                attend_v(g, 2)
                scores(g, 4, 0, gp)
                blk(1, 4, KT)
                a_transpose(g, 3)
                scores(g, 4, 1, gp)
                attend_v(g, 3)
                blk(2, 0, 6)
                a_transpose(g, 4)
                blk(2, 6, KT)
                attend_v(g, 4)
                va_transpose(hd)

            def last_head(g, gp):
                def fill(k):
                    product(B_OB // 2, 0, O_OB, 0, y_hi, y_lo, (y_ready, HEADS), O_OB, k, k + 1)
                scores(g, 0, 0, gp)
                scores(g, 0, 1, gp)
                fill(0)
                att_sum(g - 1)
                scores(g, 1, 0, gp)
                scores(g, 1, 1, gp)
                fill(1)
                a_transpose(g, 0)
                scores(g, 2, 0, gp)
                attend_v(g, 0)
                scores(g, 2, 1, gp)
                fill(2)
                a_transpose(g, 1)
                scores(g, 3, 0, gp)
                attend_v(g, 1)
                scores(g, 3, 1, gp)
                fill(3)
                a_transpose(g, 2)
                scores(g, 4, 0, gp)
                attend_v(g, 2)
                scores(g, 4, 1, gp)
                fill(4)
                a_transpose(g, 3)
                fill(5)
                attend_v(g, 3)
                a_transpose(g, 4)
                fill(6)
                attend_v(g, 4)
                att_sum(g)

            mb = B_KVQ // 2
            kvq(0, mb, 0, False, False)
            pe.wait_ge(rstd_ready, 3)
            kvq(1, mb, 1, True, False)
            with pe.Fori(1, HEADS // 2) as i:
                kvq(2 * i, mb + 3 * i, 0, True, True)
                kvq(2 * i + 1, mb + 3 * i, 1, True, True)
            last_head(HEADS - 1, 1)
            product(B_OB // 2, 0, O_OB, 0, y_hi, y_lo, (y_ready, HEADS), k0=KT - 1)
            product(B_OB // 2, 1, O_OB + 1, 1, y_hi, y_lo)
            out_model(B_OB, O_OB, HEADS, 1)
            pe.wait_ge(ao_rs, HEADS)
            ffn_up(B_UB, O_UB, 3)
            ffn_down(B_DB, O_DB, 1)
            norm_sum(4)


def tile_shape(ti):
    return (META, META, 0) if ti == 0 else (P, META + P * ti, META + P * (ti - 1))


def kernel(**inputs):
    import numpy as np
    import concourse.bacc as bacc
    from concourse.bass_utils import run_bass_kernel_spmd

    a = {k: np.asarray(v) for k, v in inputs.items()}

    def tiles_of(w):
        k, m = w.shape
        return w.reshape(k // P, P, m // P, P).transpose(2, 1, 0, 3).reshape(m // P, P, k)

    def in_blocks(w):
        t = tiles_of(w)
        t = np.concatenate([t, np.zeros((t.shape[0], P, FB * KT * P - t.shape[2]), np.float32)], axis=2)
        return t.reshape(-1, P, FB, KT * P).transpose(0, 2, 1, 3).reshape(-1, P, KT * P)

    w_in = tiles_of(a["hg_w_in"][0]).reshape(4, HEADS, P, D)
    w_kv = tiles_of(a["w_kv"]).reshape(2, HEADS, P, D)
    w_q = tiles_of(a["da_w_q"][0])

    def up(l):
        return tiles_of(a["ffn_w_up"][l]).reshape(2, FT, P, D).transpose(1, 0, 2, 3).reshape(2 * FT, P, D)

    wstream = np.concatenate([
        w_in[[1, 0, 2]].transpose(1, 0, 2, 3).reshape(3 * HEADS, P, D), w_in[3],
        tiles_of(a["hg_w_o"][0]), up(0), in_blocks(a["ffn_w_down"][0]),
        np.stack([w_kv[0], w_kv[1], w_q], axis=1).reshape(3 * HEADS, P, D),
        tiles_of(a["da_w_o"][0]), up(1), in_blocks(a["ffn_w_down"][1])])

    def cols(v):
        return v.reshape(-1, P).T

    def pairs(v):
        return cols(v.reshape(2, FT, P).transpose(1, 0, 2).reshape(-1))

    lam = np.stack([a[n][0] for n in ("da_lam_q1", "da_lam_q2", "da_lam_k1", "da_lam_k2")], axis=1)
    lam = np.concatenate([lam, np.zeros((P - DH, 4), np.float32)])
    vecs = np.concatenate(
        [cols(a["norm_mix"][0]), cols(a["norm_mix"][1]), cols(a["norm_ffn"][0]), cols(a["norm_ffn"][1]),
         cols(a["hg_lb"][0]), cols(a["hg_gain_o"][0]), cols(a["kv_norm"]), cols(a["final_norm"]),
         cols(a["da_sub_gain"][0]), lam]
        + [pairs(a["ffn_conv_w"][l, t]) for l in range(2) for t in range(3)]
        + [pairs(a["ffn_conv_b"][l]) for l in range(2)], axis=1)

    i = np.arange(P)
    keep = np.ones((P, T), np.float32)
    keep[:, 0] = 0
    keep[:, META::P] = 0
    s, t = i[:, None], i[None, :]
    masks = np.stack([(s // (2 * w) == t // (2 * w)) & ((s % (2 * w) < w) & (t % (2 * w) >= w) if w > 1 else s <= t)
                      for w in MASKED_LEVELS], axis=1).astype(np.float32)
    consts = np.concatenate([np.eye(P, dtype=np.float32),
                             np.where(i[None, :] > i[:, None], np.float32(MASKED), np.float32(0)), keep,
                             masks.reshape(P, -1)], axis=1)

    arrays = {
        "wstream": wstream,
        "xT": np.ascontiguousarray(a["x"][0].T.reshape(KT, P, SEQ).transpose(1, 0, 2)),
        "metaT": np.ascontiguousarray(a["meta_tokens"].T.reshape(KT, P, META).transpose(1, 0, 2)),
        "vecs": np.ascontiguousarray(vecs), "consts": np.ascontiguousarray(consts)}
    nc = bacc.Bacc("TRN2", target_bir_lowering=False, num_devices=1)
    aps = [nc.dram_tensor(n, v.shape, mybir.dt.from_np(v.dtype), kind="ExternalInput").ap() for n, v in arrays.items()]
    result = nc.dram_tensor("result", (KT, P, SEQ), F32, kind="ExternalOutput").ap()
    build(nc, *aps, result)
    r = run_bass_kernel_spmd(nc, [arrays], core_ids=[0])
    return r.results[0]["result"].reshape(D, SEQ).T.reshape(1, SEQ, D)
```

```python
import math
from contextlib import ExitStack

import concourse.bass as bass
from concourse import mybir

F32 = mybir.dt.float32
F32R = mybir.dt.float32r
BF16 = mybir.dt.bfloat16
U8 = mybir.dt.uint8
ALU = mybir.AluOpType
ACT = mybir.ActivationFunctionType
AX_X = mybir.AxisListType.X

P = 128
D = 1024
KT = D // P
SEQ = 512
META = 16
T = SEQ + META
TH = T // 2
HEADS = D // P
FIRST = [0, 0, 0, META - 4, META]
D_FF = 2816
FT = D_FF // P
FB = 3
POOL_TILES = [0, 1]
NC = SEQ // P
EPS = 1e-5
F_FLOOR = 1e-30
LN_SPLIT = 2.0 ** -60
MASKED = -1e30
LN, LN_EXP = "natural_log", "natural_log_exp_and_others"
LAM_INIT = 0.8 - 0.6 * math.exp(-0.3)
DH = 64
Q_SCALE = DH ** -0.5

STREAM = [("in", 4 * HEADS, 4 * HEADS), ("o_a", KT, KT), ("up_a", 2 * FT, 2 * FT), ("down_a", FB * KT, KT),
          ("kvq", 3 * HEADS, 3 * HEADS), ("o_b", KT, KT), ("up_b", 2 * FT, 2 * FT), ("down_b", FB * KT, KT)]
BLOCK0, OUT0 = {}, {}
_b = _o = 0
for _name, _nb, _no in STREAM:
    BLOCK0[_name], OUT0[_name] = _b, _o
    _b, _o = _b + _nb, _o + _no
NBLOCKS, NOUTS = _b, _o

VEC = {}
_c = 0
for _name, _w in [("norm_mix_a", KT), ("norm_mix_b", KT), ("norm_ffn_a", KT), ("norm_ffn_b", KT), ("lb", KT),
                  ("gain_o", KT), ("kv_norm", KT), ("final_norm", KT), ("sub_gain", 1), ("lam", 4),
                  ("conv_w_a", 3 * 2 * FT), ("conv_w_b", 3 * 2 * FT), ("conv_b_a", 2 * FT), ("conv_b_b", 2 * FT)]:
    VEC[_name] = _c
    _c += _w
NVEC = _c

LEVELS = [64, 32, 16, 8, 4, 2]
MASKED_LEVELS = [16, 8, 4, 2, 1]


def build(nc, wstream, xT, metaT, vecs, consts, out):
    address = [(nc.sbuf_base + 63) // 64 * 64]

    def place(name, shape, dt=F32, at=address):
        size = mybir.dt.size(dt)
        for s in shape[1:]:
            size *= s
        t = nc.alloc_sbuf_tensor_at(name, shape, dt, offset=at[0])
        at[0] += (size + 31) // 32 * 32
        return t

    ctx = ExitStack()
    with ctx:
        def sem(name):
            return ctx.enter_context(nc.semaphore(name))

        h = place("h", [P, KT, T])
        x_hi = place("x_hi", [P, KT, T], F32R)
        x_lo = place("x_lo", [P, KT, T], F32R)
        w_raw = place("w_raw", [P, 2, KT * P])
        w_hi = place("w_hi", [P, 2, KT * P], F32R)
        w_lo = place("w_lo", [P, 2, KT * P], F32R)
        rstd = place("rstd", [P, T])
        lntmp = place("lntmp", [P, T])
        sqb = place("sqb", [P, 2, T])
        sqsum = place("sqsum", [P, T])
        vec = place("vec", [P, NVEC])
        cst = place("cst", [P, 2 * P + T])
        msk_f = place("msk_f", [P, len(MASKED_LEVELS), P])
        msk = place("msk", [P, len(MASKED_LEVELS), P], U8)
        ones = place("ones", [P, P])
        ident_b = place("ident_b", [P, P], BF16)
        causal_b = place("causal_b", [P, P], BF16)
        small = place("small", [P, 64])
        ident, causal, chunk_keep = cst[:, 0:P], cst[:, P:2 * P], cst[:, 2 * P:2 * P + T]
        eps_c, nlam, sub_c, nlr = (small[:, i:i + 1] for i in range(4))
        carry, zero_c = small[:, 60:61], small[:, 61:62]
        lb_c, oml_c, noml_c, tmp_c, tmp2_c = (small[:, 8 * i:8 * i + 8] for i in range(1, 6))
        lamv, lame = small[0:DH, 48:50], small[:, 50:52]
        nmax, esum, rsum = small[:, 52:54], small[:, 54:56], small[:, 56:58]

        f_at = address[0]
        ub = [place(f"ub{j}", [P, T + 8]) for j in range(2)]
        cb = [place(f"cb{j}", [P, T]) for j in range(2)]
        sa = place("sa", [P, T])
        am = place("am", [P, T])
        f_end = address[0]
        at = [f_at]
        att = place("att", [P, NC, P], at=at)
        v_t = place("v_t", [P, NC, P], at=at)
        k_t = place("k_t", [P, NC - 1, P], at=at)
        state = place("state", [P, NC, P], at=at)
        k_meta_t = place("k_meta_t", [META, P], at=at)
        v_meta_t = place("v_meta_t", [META, P], at=at)
        att_meta = place("att_meta", [META, META], at=at)
        dec = place("dec", [P, 8], at=at)
        assert at[0] <= f_end
        at = [f_at]
        prob = [place(f"prob{c}", [P, T], at=at) for c in range(2)]
        attn = place("attn", [P, T], at=at)
        o_att = [place("o_att0", [P, T], at=at)]
        rs_att = place("rs_att", [P, T], at=at)
        attn_mt = place("attn_mt", [META, P], at=at)
        v_meta_h = place("v_meta_h", [META, P], at=at)
        assert at[0] <= f_end

        r_at = address[0]
        act_hi = place("act_hi", [P, FT, T], F32R)
        act_lo = place("act_lo", [P, FT, T], F32R)
        r_end = address[0]
        assert r_end <= nc.sbuf_usable_end, r_end
        at = [r_at]
        y_hi = place("y_hi", [P, KT, T], F32R, at=at)
        y_lo = place("y_lo", [P, KT, T], F32R, at=at)
        mixer_at = at[0]
        oo = place("oo", [P, KT, T], at=at)
        zf, zq, zv = (place(f"z{n}", [P, T], at=at) for n in "fqv")
        kk = place("kk", [P, T], at=at)
        qq = place("qq", [P, T], at=at)
        lf = place("lf", [P, T], at=at)
        lf2 = place("lf2", [P, T], at=at)
        fg = place("fg", [P, T], at=at)
        bb = place("bb", [P, T], at=at)
        qe = place("qe", [P, T], at=at)
        ks = place("ks", [P, T], at=at)
        lev = place("lev", [P, len(LEVELS), T], at=at)
        osq = place("osq", [P, T], at=at)
        rs = place("rs", [P, T], at=at)
        zg, sig_g = (zf, zq, zv), (fg, lf, lf2)
        assert at[0] <= r_end, (at[0], r_end)
        at = [mixer_at]
        xq_hi = place("xq_hi", [P, KT, T], F32R, at=at)
        xq_lo = place("xq_lo", [P, KT, T], F32R, at=at)
        zkq = place("zkq", [P, T], at=at)
        kh_hi = [place(f"kh_hi{j}", [P, T], F32R, at=at) for j in range(2)]
        kh_lo = [place(f"kh_lo{j}", [P, T], F32R, at=at) for j in range(2)]
        qh_hi, qh_lo = (place(f"qh_{n}", [P, T], F32R, at=at) for n in ("hi", "lo"))
        zva = place("zva", [P, T], at=at)
        v_h = place("v_h", [P, NC, P], at=at)
        attn_t = place("attn_t", [P, NC, P], at=at)
        osq_att = place("osq_att", [P, T], at=at)
        o_att.append(place("o_att1", [P, T], at=at))
        assert at[0] <= r_end, (at[0], r_end)

        prod = ctx.enter_context(nc.psum_tensor("prod", [P, 2, 2, 512], F32))
        mix = ctx.enter_context(nc.psum_tensor("mix", [P, 4, 512], F32))

        def halves(t):
            return t.rearrange("p (a b) -> p a b", a=2)

        def out_ps(s, t0=0):
            return prod[:, s, :, 0:(T - t0) // 2]

        def main(t):
            return t[:, META:T]

        def blocks(t, c):
            return (t[:, 0:T] if c <= 8 else main(t)).rearrange("p (n w) -> p n w", w=2 * c)

        h_loaded = [sem(f"h_loaded{k}") for k in range(KT)]
        vec_loaded, meta_loaded, consts_loaded, stored = (
            sem(n) for n in ("vec_loaded", "meta_loaded", "consts_loaded", "stored"))
        raw_in = [sem(f"raw_in{s}") for s in range(2)]
        hi_ready, lo_ready, block_done, drained = sem("hi_ready"), sem("lo_ready"), sem("block_done"), sem("drained")
        ones_set, att_zero = sem("ones_set"), sem("att_zero")
        bf_ready, lb_step, lb_exp, lam_prod, lam_sum, lam_exp, lam_step = (
            sem(n) for n in ("bf_ready", "lb_step", "lb_exp", "lam_prod", "lam_sum", "lam_exp", "lam_step"))
        x_hi_done, x_ready, sq_done, sq_added, ms_done, ln_done, rstd_ready = (
            sem(n) for n in ("x_hi_done", "x_ready", "sq_done", "sq_added", "ms_done", "ln_done", "rstd_ready"))
        sig_done, f_done, k_done, clip_done, lnf_done, q_done, lf_done, b_done = (
            sem(n) for n in ("sig_done", "f_done", "k_done", "clip_done", "lnf_done", "q_done", "lf_done", "b_done"))
        qe_exp, ks_exp, dec_done, qe_done, ks_done, sub_done, lev_exp, lev_done, one_exp, one_done = (
            sem(n) for n in ("qe_exp", "ks_exp", "dec_done", "qe_done", "ks_done", "sub_done", "lev_exp", "lev_done",
                             "one_exp", "one_done"))
        vt_done, vt_copied, kt_done, kt_copied, u_done, s_done = (
            sem(n) for n in ("vt_done", "vt_copied", "kt_done", "kt_copied", "u_done", "s_done"))
        lp_done, lp_copied, lp_taken, lm_done, lm_taken = (
            sem(n) for n in ("lp_done", "lp_copied", "lp_taken", "lm_done", "lm_taken"))
        o_done, o_copied, osq_done, os_done, os_ln, rs_done, gate_done, y1_done, y2_done, y_hi_done, y_ready = (
            sem(n) for n in ("o_done", "o_copied", "osq_done", "os_done", "os_ln", "rs_done", "gate_done", "y1_done",
                             "y2_done", "y_hi_done", "y_ready"))
        base_done, tap_done, conv_done, silu_done, am_done, act_hi_done, act_ready = (
            sem(n) for n in ("base_done", "tap_done", "conv_done", "silu_done", "am_done", "act_hi_done", "act_ready"))
        pad_zero, mask_ready = sem("pad_zero"), sem("mask_ready")
        xq_hi_done, xq_ready, s_up, max_done, exp_done, rec_done, scaled, comb_done = (
            sem(n) for n in ("xq_hi_done", "xq_ready", "s_up", "max_done", "exp_done", "rec_done", "scaled", "comb_done"))
        kq_hi_done, kq_ready = sem("kq_hi_done"), sem("kq_ready")
        at_done, at_copied, pv_done, pv_copied, va_done, va_copied = (
            sem(n) for n in ("at_done", "at_copied", "pv_done", "pv_copied", "va_done", "va_copied"))
        ao_sq, ao_sum, ao_ln, ao_rs, ao_y = (sem(n) for n in ("ao_sq", "ao_sum", "ao_ln", "ao_rs", "ao_y"))
        gained, out_ready, out_pool = sem("gained"), sem("out_ready"), sem("out_pool")

        B_IN, B_OA, B_UA, B_DA, B_KVQ, B_OB, B_UB, B_DB = (BLOCK0[n] for n, _, _ in STREAM)
        O_IN, O_OA, O_UA, O_DA, O_KVQ, O_OB, O_UB, O_DB = (OUT0[n] for n, _, _ in STREAM)

        def need(eng, s, value):
            if not (isinstance(value, int) and value <= 0):
                eng.wait_ge(s, value)

        block = ctx.enter_context(nc.Block())

        @block.sync
        def _(sp):
            sp.dma_start(w_raw[:, 0, :], wstream[0]).then_inc(raw_in[0], 16)
            sp.dma_start(vec[:, 0:KT], vecs[:, 0:KT]).then_inc(vec_loaded, 16)
            sp.dma_start(h[:, :, 0:META], metaT).then_inc(meta_loaded, 16)
            for k in range(KT):
                sp.dma_start(h[:, k, META:T], xT[:, k, :]).then_inc(h_loaded[k], 16)
                if k == 3:
                    sp.dma_start(w_raw[:, 1, :], wstream[1]).then_inc(raw_in[1], 16)
            sp.dma_start(vec[:, KT:NVEC], vecs[:, KT:NVEC]).then_inc(consts_loaded, 16)
            sp.dma_start(cst[:, :], consts[:, 0:2 * P + T]).then_inc(consts_loaded, 16)
            sp.dma_start(msk_f[:, :, :], consts[:, 2 * P + T:].rearrange("p (a b) -> p a b", b=P)).then_inc(consts_loaded, 16)
            with sp.Fori(1, NBLOCKS // 2) as m:
                for s in range(2):
                    sp.wait_ge(lo_ready, 2 * m + s - 1)
                    sp.dma_start(w_raw[:, s, :], wstream[2 * m + s]).then_inc(raw_in[s], 16)
            dve_tiles = [k for k in range(KT) if k not in POOL_TILES]
            for k in dve_tiles[:2] + POOL_TILES[:1] + dve_tiles[2:4] + POOL_TILES[1:] + dve_tiles[4:]:
                if k in POOL_TILES:
                    sp.wait_ge(out_pool, POOL_TILES.index(k) + 1)
                else:
                    sp.wait_ge(out_ready, dve_tiles.index(k) + 1)
                sp.dma_start(out[k], h[:, k, META:T]).then_inc(stored, 16)
            sp.wait_ge(stored, 16 * KT)

        @block.gpsimd
        def _(pool):
            pool.memset(ones[:, :], 1.0).then_inc(ones_set, 1)
            pool.memset(eps_c, EPS).then_inc(ones_set, 1)
            pool.memset(zero_c, 0.0).then_inc(ones_set, 1)
            pool.memset(att[:, :, :], 0.0).then_inc(att_zero, 1)
            pool.memset(att_meta[:, :], 0.0).then_inc(att_zero, 1)

            def norm_add(n):
                t0 = FIRST[n]
                for k in range(KT if n < 4 else KT - 1):
                    pool.wait_ge(sq_done, KT * n + k + 1)
                    if k == 0:
                        need(pool, ms_done, n)
                        pool.tensor_copy(sqsum[:, t0:T], sqb[:, 0, t0:T]).then_inc(sq_added, 1)
                    else:
                        pool.wait_ge(sq_added, KT * n + k)
                        pool.tensor_tensor(sqsum[:, t0:T], sqsum[:, t0:T], sqb[:, k % 2, t0:T], ALU.add).then_inc(sq_added, 1)

            def level_subs(c):
                pool.wait_ge(b_done, c)
                need(pool, lm_done, c - 1)
                for i, w in enumerate(LEVELS):
                    b3, l3 = blocks(bb, w), blocks(lev[:, i, :], w)
                    ref = b3[:, :, w - 1:w].broadcast_to([P, b3.shape[1], w])
                    pool.tensor_tensor(l3[:, :, 0:w], ref, b3[:, :, 0:w], ALU.subtract)
                    pool.tensor_tensor(l3[:, :, w:2 * w], b3[:, :, w:2 * w], ref, ALU.subtract).then_inc(sub_done, 1)

            norm_add(0)
            level_subs(1)
            with pool.Fori(2, HEADS + 1) as c:
                level_subs(c)
            for n in range(1, 5):
                norm_add(n)
            pool.wait_ge(rstd_ready, 5)
            for k in POOL_TILES:
                pool.wait_ge(gained, k + 1)
                pool.tensor_tensor(h[:, k, META:T], h[:, k, META:T], rstd[:, META:T], ALU.mult).then_inc(out_pool, 1)

        @block.scalar
        def _(act):
            def split(m, s):
                act.wait_ge(raw_in[s], 16 * m + 16)
                need(act, block_done, 2 * m + s - 1)
                act.activation(w_hi[:, s, :], w_raw[:, s, :], ACT.Copy).then_inc(hi_ready, 1)

            def norm_tile(n, k, s, gain):
                t0 = FIRST[n]
                if n:
                    act.wait_ge(sq_added, KT * n + k - 1)
                act.activation(x_hi[:, k, t0:T], h[:, k, t0:T], ACT.Copy,
                               scale=vec[:, bass.ds(VEC[gain] + k, 1)]).then_inc(x_hi_done, 1)
                if n == 0:
                    need(act, sq_added, k - 1)
                act.activation(sqb[:, s, t0:T], h[:, k, t0:T], ACT.Square).then_inc(sq_done, 1)

            def norm_rstd(n, outs):
                act.wait_ge(ms_done, n + 1)
                need(act, rstd_ready, n)
                t0 = FIRST[n]
                act.activation(halves(lntmp[:, t0:T]), mix[:, 0:2, 0:(T - t0) // 2], ACT.Ln, bias=eps_c,
                               scale=1.0 / D).then_inc(ln_done, 1)
                act.wait_ge(ln_done, n + 1)
                need(act, drained, outs)
                act.activation(rstd[:, t0:T], lntmp[:, t0:T], ACT.Exp, scale=-0.5).then_inc(rstd_ready, 1)

            split(0, 0)
            act.wait_ge(vec_loaded, 16)
            act.wait_ge(meta_loaded, 16)
            act.wait_ge(ones_set, 3)
            for k in range(KT):
                act.wait_ge(h_loaded[k], 16)
                norm_tile(0, k, k % 2, "norm_mix_a")
                if k == 4:
                    split(0, 1)
            act.preload_act_table_set(LN_EXP)
            split(1, 0)
            norm_rstd(0, 0)
            act.wait_ge(consts_loaded, 48)
            act.activation(ident_b[:, :], ident, ACT.Copy).then_inc(bf_ready, 1)
            act.activation(causal_b[:, :], causal, ACT.Copy).then_inc(bf_ready, 1)
            act.wait_ge(lb_step, 1)
            act.activation(tmp_c, tmp_c, ACT.Exp).then_inc(lb_exp, 1)
            act.wait_ge(lam_sum, 1)
            act.activation(lame, mix[:, 2, 0:2], ACT.Exp).then_inc(lam_exp, 1)

            def gla_sigmoids(hd):
                act.wait_ge(drained, 3 * hd + 2)
                act.activation(zf[:, :], zf[:, :], ACT.Sigmoid).then_inc(sig_done, 1)
                need(act, kt_done, hd)
                act.activation(ks[:, :], zq[:, :], ACT.Sigmoid).then_inc(sig_done, 1)

            def gla_ln(c):
                act.wait_ge(clip_done, 2 * c)
                act.activation(lf[:, :], lf[:, :], ACT.Ln).then_inc(lnf_done, 1)
                act.activation(lf2[:, :], lf2[:, :], ACT.Ln, scale=1.0 / LN_SPLIT).then_inc(lnf_done, 1)

            def copy_vt(c):
                act.wait_ge(vt_done, c)
                act.activation(v_t[:, :, :], mix[:, 2, :].rearrange("p (a b) -> p a b", b=P), ACT.Copy)
                act.activation(v_meta_t[:, :], mix[0:META, 3, 0:P], ACT.Copy).then_inc(vt_copied, 1)

            def ks_exps(c):
                need(act, s_done, NC * (c - 1))
                act.wait_ge(b_done, c)
                act.activation(dec[:, 0:NC - 1], bb[:, META + P - 1:T - 1:P], ACT.Exp).then_inc(dec_done, 1)
                act.wait_ge(q_done, c)
                act.activation(ks[:, 0:META], bb[:, 0:META], ACT.Exp, bias=bb[:, META - 1:META], scale=-1.0)
                for j in range(NC - 1):
                    a = META + j * P
                    last = act.activation(ks[:, a:a + P], bb[:, a:a + P], ACT.Exp,
                                          bias=bb[:, a + P - 1:a + P], scale=-1.0)
                last.then_inc(ks_exp, 1)

            def qe_exps(c):
                need(act, o_done, c - 1)
                act.activation(main(qe), main(bb), ACT.Exp).then_inc(qe_exp, 1)

            def gla_level(c, i):
                nl = len(LEVELS)
                act.wait_ge(sub_done, nl * (c - 1) + i + 1)
                part = lev[:, i, :] if LEVELS[i] <= 8 else lev[:, i, META:T]
                act.activation(part, part, ACT.Exp).then_inc(lev_exp, 1)

            def gla_one(c):
                act.activation(lf2[:, 0:TH], lf[:, 1::2], ACT.Exp)
                act.activation(lf2[:, TH:T], lf[:, 1::2], ACT.Exp, scale=-1.0).then_inc(one_exp, 1)

            def copy_kt(c):
                act.wait_ge(kt_done, c)
                act.activation(k_t[:, :, :], mix[:, 2, 0:(NC - 1) * P].rearrange("p (a b) -> p a b", b=P), ACT.Copy)
                act.activation(k_meta_t[:, :], mix[0:META, 3, P:2 * P], ACT.Copy).then_inc(kt_copied, 1)

            def copy_level64(c):
                need(act, o_done, c - 1)
                act.wait_ge(lp_done, 7 * (c - 1) + 1)
                act.activation(att[0:64, :, 64:128], mix[0:64, 0, 0:NC * 64].rearrange("p (a b) -> p a b", b=64),
                               ACT.Copy).then_inc(lp_copied, 1)

            def copy_level32(c):
                act.wait_ge(lp_done, 7 * (c - 1) + 2)
                for a in (0, 64):
                    last = act.activation(att[a:a + 32, :, a + 32:a + 64],
                                          mix[a:a + 32, 1, 0:NC * 32].rearrange("p (a b) -> p a b", b=32), ACT.Copy)
                last.then_inc(lp_copied, 1)

            def out_copy(c):
                act.wait_ge(o_done, c)
                need(act, os_done, c - 1)
                act.activation(main(osq), mix[:, 2, :], ACT.Square)
                act.activation(osq[:, 0:META], mix[:, 3, 0:META], ACT.Square).then_inc(osq_done, 1)
                act.activation(oo[:, c - 1, META:T], mix[:, 2, :], ACT.Copy)
                act.activation(oo[:, c - 1, 0:META], mix[:, 3, 0:META], ACT.Copy).then_inc(o_copied, 1)

            def out_rstd(c):
                act.wait_ge(os_done, c)
                need(act, y1_done, c - 1)
                act.activation(halves(rs[:, :]), mix[:, 0:2, 0:TH], ACT.Ln, bias=eps_c, scale=1.0 / P).then_inc(os_ln, 1)
                act.wait_ge(os_ln, c)
                act.activation(rs[:, :], rs[:, :], ACT.Exp, scale=-0.5).then_inc(rs_done, 1)

            def gate_sigmoid(j):
                act.wait_ge(drained, 3 * HEADS + j + 1)
                if j < 3:
                    act.wait_ge(one_done, HEADS)
                need(act, y2_done, j - 2)
                act.activation(sig_g[j % 3][:, :], zg[j % 3][:, :], ACT.Sigmoid).then_inc(sig_done, 1)

            def out_hi(j):
                act.wait_ge(y2_done, j + 1)
                act.activation(y_hi[:, j, :], oo[:, j, :], ACT.Copy).then_inc(y_hi_done, 1)

            def head(hd, m, par, gla, fin, last=False):
                def nxt(j):
                    q = 3 * par + j + 2
                    split(m + q // 2, q % 2)
                if gla:
                    gla_ln(hd)
                    nxt(0)
                    act.preload_act_table_set(LN_EXP)
                    gla_level(hd, 0)
                if fin:
                    out_copy(hd - 1)
                if gla:
                    gla_level(hd, 1)
                    qe_exps(hd)
                    ks_exps(hd)
                    gla_level(hd, 2)
                if fin:
                    out_rstd(hd - 1)
                if gla:
                    gla_level(hd, 3)
                    copy_vt(hd)
                    gla_level(hd, 4)
                    gla_level(hd, 5)
                if gla:
                    copy_level64(hd)
                    copy_level32(hd)
                nxt(1)
                if gla:
                    copy_kt(hd)
                    gla_one(hd)
                if last:
                    for j in range(2):
                        gate_sigmoid(j)
                else:
                    gla_sigmoids(hd)
                nxt(2)
                if not last:
                    act.preload_act_table_set(LN)

            head(0, 0, 0, False, False)
            head(1, 0, 1, True, False)
            with act.Fori(1, HEADS // 2) as i:
                head(2 * i, 3 * i, 0, True, True)
                head(2 * i + 1, 3 * i, 1, True, True)
            head(HEADS, 3 * HEADS // 2, 0, True, True, True)
            gate_sigmoid(2)
            out_hi(0)
            out_hi(1)
            for j in range(3, HEADS):
                n = 3 * HEADS + j + 2
                if j == 3:
                    out_copy(HEADS)
                split(n // 2, n % 2)
                gate_sigmoid(j)
                out_hi(j - 1)
                if j == 4:
                    act.preload_act_table_set(LN_EXP)
                    out_rstd(HEADS)
            out_hi(HEADS - 1)
            act.preload_act_table_set(LN_EXP)

            def out_phase(b0, o0, per, n, gain):
                with act.Fori(0, KT // 2) as i:
                    for s in range(2):
                        for j in range(per):
                            q = per * s + j
                            split(b0 // 2 + per * i + (q + 2) // 2, q % 2)
                        act.wait_ge(drained, o0 + 2 * i + s + 1)
                        norm_tile(n, 2 * i + s, s, gain)

            def ffn_up(b0, o0, f, n):
                cw, cbias = VEC[f"conv_w_{'ab'[f]}"], VEC[f"conv_b_{'ab'[f]}"]
                m0 = META * f

                def tail_hi(p):
                    act.wait_ge(am_done, FT * f + p + 1)
                    act.wait_ge(consts_loaded, 48)
                    act.activation(act_hi[:, p, m0:T], am[:, m0:T], ACT.Copy).then_inc(act_hi_done, 1)

                def pair(p, prev):
                    for j in range(2):
                        split(b0 // 2 + p + 1, j)
                        if j == 0 and not prev:
                            norm_rstd(n, o0)
                        ft = 2 * p + j
                        act.wait_ge(drained, o0 + ft + 1)
                        need(act, am_done, FT * f + p)
                        act.wait_ge(consts_loaded, 48)
                        act.activation(cb[j][:, m0:T], ub[j][:, m0 + 2:T + 2], ACT.Identity, bias=vec[:, bass.ds(cbias + ft, 1)],
                                       scale=vec[:, bass.ds(cw + 2 * 2 * FT + ft, 1)]).then_inc(base_done, 1)
                        if j == 0:
                            if prev:
                                tail_hi(p - 1)
                        else:
                            act.wait_ge(conv_done, 2 * FT * f + 2 * p + 1)
                            act.activation(sa[:, m0:T], cb[0][:, m0:T], ACT.Silu).then_inc(silu_done, 1)

                pair(0, False)
                with act.Fori(1, FT) as p:
                    pair(p, True)
                tail_hi(FT - 1)

            out_phase(B_OA, O_OA, 1, 1, "norm_ffn_a")
            ffn_up(B_UA, O_UA, 0, 1)
            act.preload_act_table_set(LN_EXP)
            out_phase(B_DA, O_DA, FB, 2, "kv_norm")

            norm_rstd(2, O_DA)

            def xq_part(k0, k1):
                for k in range(k0, k1):
                    act.activation(xq_hi[:, k, :], h[:, k, :], ACT.Copy,
                                   scale=vec[:, VEC["norm_mix_b"] + k:VEC["norm_mix_b"] + k + 1]).then_inc(xq_hi_done, 1)

            act.wait_ge(block_done, B_KVQ)
            xq_part(0, KT // 2)
            def soft_exp(g, ti, c):
                nq, n, _ = tile_shape(ti)
                act.wait_ge(max_done, 10 * g + 2 * ti + c + 1)
                need(act, comb_done, 5 * g + ti)
                src = mix[0:nq, 2 * c, 0:n] if n <= 512 else mix[0:nq, 2 * c:2 * c + 2, 0:TH]
                dst = prob[c][0:nq, 0:n] if n <= 512 else halves(prob[c][0:nq, :])
                act.activation(dst, src, ACT.Exp, bias=nmax[0:nq, c:c + 1],
                               accum_out=esum[0:nq, c:c + 1]).then_inc(exp_done, 1)

            def at_copy(g, ti):
                nq, _, _ = tile_shape(ti)
                act.wait_ge(at_done, 5 * g + ti + 1)
                need(act, pv_done, 5 * g + ti)
                if ti:
                    act.activation(attn_t[:, 0:ti, :], prod[:, 1, 0, 0:ti * P].rearrange("p (a b) -> p a b", b=P), ACT.Copy)
                act.activation(attn_mt[:, 0:nq], prod[0:META, 1, 1, 0:nq], ACT.Copy).then_inc(at_copied, 1)

            def pv_copy(g, ti, par):
                nq, _, q0 = tile_shape(ti)
                act.wait_ge(pv_done, 5 * g + ti + 1)
                if ti == 0:
                    need(act, y_ready, HEADS + g - 1)
                act.activation(o_att[par][:, q0:q0 + nq], prod[:, 1, 1, P:P + nq], ACT.Copy).then_inc(pv_copied, 1)

            def att_square(g, par):
                act.wait_ge(pv_copied, 5 * g + 5)
                need(act, ao_sum, g)
                act.activation(osq_att[:, :], o_att[par][:, :], ACT.Square).then_inc(ao_sq, 1)

            def att_rstd(g):
                act.wait_ge(ao_sum, g + 1)
                need(act, ao_y, g)
                for a in range(2):
                    last = act.activation(rs_att[:, a * TH:(a + 1) * TH], mix[:, 2 * a + 1, 0:TH], ACT.Ln, bias=eps_c,
                                          scale=1.0 / P)
                last.then_inc(ao_ln, 1)
                act.wait_ge(ao_ln, g + 1)
                act.activation(rs_att[:, :], rs_att[:, :], ACT.Exp, scale=-0.5).then_inc(ao_rs, 1)

            def att_hi(g, par):
                act.wait_ge(ao_y, g + 1)
                act.wait_ge(consts_loaded, 48)
                act.activation(y_hi[:, g, :], o_att[par][:, :], ACT.Copy).then_inc(y_hi_done, 1)

            def kq_hi(hd, j, dst):
                act.wait_ge(drained, O_KVQ + 3 * hd + 1 + 2 * j)
                act.activation(dst[:, :], zkq[:, :], ACT.Copy).then_inc(kq_hi_done, 1)

            def v_copy(hd):
                act.wait_ge(va_done, hd + 1)
                act.activation(v_h[:, :, :], prod[:, 1, 0, :].rearrange("p (a b) -> p a b", b=P), ACT.Copy)
                act.activation(v_meta_h[:, :], prod[0:META, 1, 1, 0:P], ACT.Copy).then_inc(va_copied, 1)

            def kvq(hd, m, par, blocks_too, attend, fin):
                def nxt(j):
                    q = 3 * par + j + 2
                    split(m + q // 2, q % 2)
                g, gp, gg = hd - 1, 1 - par, hd - 2
                if attend:
                    soft_exp(g, 0, 0)
                    soft_exp(g, 0, 1)
                    soft_exp(g, 1, 0)
                    soft_exp(g, 1, 1)
                    if blocks_too:
                        nxt(-1)
                    at_copy(g, 0)
                    soft_exp(g, 2, 0)
                    pv_copy(g, 0, gp)
                    soft_exp(g, 2, 1)
                    at_copy(g, 1)
                if blocks_too:
                    nxt(0)
                if not attend:
                    xq_part(KT // 2, KT)
                if attend:
                    pv_copy(g, 1, gp)
                if fin:
                    att_rstd(gg)
                if attend:
                    soft_exp(g, 3, 0)
                    soft_exp(g, 3, 1)
                    at_copy(g, 2)
                    pv_copy(g, 2, gp)
                    if not blocks_too:
                        att_hi(gg, par)
                if blocks_too:
                    kq_hi(hd, 0, kh_hi[par])
                if attend:
                    soft_exp(g, 4, 0)
                    at_copy(g, 3)
                if blocks_too:
                    if fin:
                        att_hi(gg, par)
                    nxt(1)
                if attend:
                    soft_exp(g, 4, 1)
                    pv_copy(g, 3, gp)
                    at_copy(g, 4)
                    if not blocks_too:
                        nxt(-1)
                    pv_copy(g, 4, gp)
                if blocks_too:
                    kq_hi(hd, 1, qh_hi)
                if attend:
                    att_square(g, gp)
                if blocks_too:
                    v_copy(hd)

            mb = B_KVQ // 2
            kvq(0, mb, 0, True, False, False)
            kvq(1, mb, 1, True, True, False)
            with act.Fori(1, HEADS // 2) as i:
                kvq(2 * i, mb + 3 * i, 0, True, True, True)
                kvq(2 * i + 1, mb + 3 * i, 1, True, True, True)
            kvq(HEADS, mb + 3 * HEADS // 2, 0, False, True, True)
            att_rstd(HEADS - 1)
            att_hi(HEADS - 1, 1)

            out_phase(B_OB, O_OB, 1, 3, "norm_ffn_b")
            ffn_up(B_UB, O_UB, 1, 3)
            act.preload_act_table_set(LN_EXP)
            for m in range(KT):
                for j in range(FB):
                    q = FB * m + j + 2
                    if q < FB * KT:
                        split(B_DB // 2 + q // 2, q % 2)
                act.wait_ge(drained, O_DB + m + 1)
                act.wait_ge(sq_added, KT * 4 + m - 1)
                act.activation(sqb[:, m % 2, META:T], h[:, m, META:T], ACT.Square).then_inc(sq_done, 1)
                if m in POOL_TILES:
                    act.wait_ge(sq_done, KT * 4 + m + 1)
                    act.activation(h[:, m, META:T], h[:, m, META:T], ACT.Copy,
                                   scale=vec[:, VEC["final_norm"] + m:VEC["final_norm"] + m + 1]).then_inc(gained, 1)
            norm_rstd(4, NOUTS)

        @block.vector
        def _(dve):
            def split(m, s):
                dve.wait_ge(hi_ready, 2 * m + s + 1)
                dve.tensor_tensor(w_lo[:, s, :], w_raw[:, s, :], w_hi[:, s, :].bitcast(F32), ALU.subtract).then_inc(lo_ready, 1)

            def norm_tile(n, k, gain):
                dve.wait_ge(x_hi_done, KT * n + k + 1)
                t0 = FIRST[n]
                dve.scalar_tensor_tensor(x_lo[:, k, t0:T], h[:, k, t0:T], vec[:, bass.ds(VEC[gain] + k, 1)],
                                         x_hi[:, k, t0:T].bitcast(F32), ALU.mult, ALU.subtract).then_inc(x_ready, 1)

            def scaled_out(dst, s, block_no, scale=None, t0=0):
                dve.wait_ge(block_done, block_no)
                if scale is None:
                    dve.tensor_tensor(halves(dst), out_ps(s, t0), halves(rstd[:, t0:T]), ALU.mult).then_inc(drained, 1)
                else:
                    dve.scalar_tensor_tensor(halves(dst), out_ps(s), scale, halves(rstd[:, :]),
                                             ALU.mult, ALU.mult).then_inc(drained, 1)

            split(0, 0)
            dve.wait_ge(vec_loaded, 16)
            for k in range(KT):
                norm_tile(0, k, "norm_mix_a")
                if k == 4:
                    split(0, 1)
            dve.wait_ge(consts_loaded, 48)
            lbp = vec[:, VEC["lb"]:VEC["lb"] + KT]
            dve.tensor_tensor(tmp_c, lbp, lbp, ALU.subtract).then_inc(lb_step, 1)
            v0 = VEC["lam"]
            dve.tensor_tensor(lamv, vec[0:DH, v0:v0 + 2], vec[0:DH, v0 + 2:v0 + 4], ALU.mult).then_inc(lam_prod, 1)
            dve.tensor_single_scalar(sub_c, vec[:, VEC["sub_gain"]:VEC["sub_gain"] + 1], 1.0 - LAM_INIT, ALU.mult)
            dve.tensor_copy(msk[:, :, :], msk_f[:, :, :]).then_inc(mask_ready, 1)
            split(1, 0)
            dve.wait_ge(rstd_ready, 1)

            def evac(hd, j, dst):
                b = 4 * hd + j + 1
                scaled_out(dst, j % 2, b)

            def gla_gates(c):
                g = c - 1
                need(dve, lm_done, g)
                dve.wait_ge(sig_done, 2 * g + 1)
                dve.tensor_scalar(fg[:, :], zf[:, :], oml_c[:, bass.ds(g, 1)], lb_c[:, bass.ds(g, 1)],
                                  ALU.mult, ALU.add).then_inc(f_done, 1)
                dve.tensor_scalar(kk[:, :], zf[:, :], noml_c[:, bass.ds(g, 1)], oml_c[:, bass.ds(g, 1)],
                                  ALU.mult, ALU.add).then_inc(k_done, 1)
                dve.wait_ge(f_done, c)
                dve.tensor_single_scalar(lf[:, :], fg[:, :], LN_SPLIT, ALU.max).then_inc(clip_done, 1)
                dve.tensor_scalar(lf2[:, :], fg[:, :], LN_SPLIT, F_FLOOR, ALU.min, ALU.max).then_inc(clip_done, 1)
                dve.wait_ge(sig_done, 2 * g + 2)
                dve.tensor_tensor(qq[:, :], zq[:, :], ks[:, :], ALU.mult).then_inc(q_done, 1)

            def decays(c):
                dve.wait_ge(lnf_done, 2 * c)
                dve.tensor_tensor(lf[:, :], lf[:, :], lf2[:, :], ALU.add).then_inc(lf_done, 1)
                dve.wait_ge(lf_done, c)
                dve.tensor_tensor_scan(bb[:, :], chunk_keep, lf[:, :], 0.0, ALU.mult, ALU.add).then_inc(b_done, 1)

            def level_mul(c, i):
                w = LEVELS[i]
                dve.wait_ge(lev_exp, len(LEVELS) * (c - 1) + i + 1)
                l3, k3, q3 = blocks(lev[:, i, :], w), blocks(kk, w), blocks(qq, w)
                dve.tensor_tensor(l3[:, :, 0:w], l3[:, :, 0:w], k3[:, :, 0:w], ALU.mult)
                dve.tensor_tensor(l3[:, :, w:2 * w], l3[:, :, w:2 * w], q3[:, :, w:2 * w], ALU.mult).then_inc(lev_done, 1)

            def ks_mul(c):
                dve.wait_ge(ks_exp, c)
                dve.tensor_tensor(ks[:, 0:T - P], ks[:, 0:T - P], kk[:, 0:T - P], ALU.mult).then_inc(ks_done, 1)

            def qe_mul(c):
                dve.wait_ge(qe_exp, c)
                dve.tensor_tensor(main(qe), main(qe), main(qq), ALU.mult).then_inc(qe_done, 1)

            def level_one(c):
                dve.wait_ge(one_exp, c)
                dve.wait_ge(lev_done, len(LEVELS) * c)
                dve.tensor_tensor(qq[:, 1::2], qq[:, 1::2], lf2[:, 0:TH], ALU.mult)
                dve.tensor_tensor(kk[:, 1::2], kk[:, 1::2], lf2[:, TH:T], ALU.mult).then_inc(one_done, 1)

            def take_level(c, i):
                dve.wait_ge(mask_ready, 1)
                if i == 0:
                    need(dve, o_done, c - 1)
                    need(dve, lm_taken, 4 * (c - 1))
                    dve.wait_ge(lp_copied, 2 * c)
                need(dve, lp_taken, 5 * (c - 1) + i)
                dve.wait_ge(lp_done, 7 * (c - 1) + 3 + i)
                dve.tensor_copy(carry, zero_c)
                m = msk[:, i:i + 1, :].broadcast_to([P, NC, P])
                dve.copy_predicated(att[:, :, :], m, mix[:, i % 2, :].rearrange("p (a b) -> p a b", b=P)).then_inc(lp_taken, 1)

            def take_meta(c):
                dve.wait_ge(lm_done, c)
                dve.wait_ge(lp_taken, 5 * c)
                for i in range(1, 5):
                    need(dve, lm_taken, 4 * (c - 1) + i - 1)
                    dve.tensor_copy(carry, zero_c)
                    dve.copy_predicated(att_meta[:, :], msk[0:META, i, 0:META],
                                        mix[0:META, 3, 2 * P + META * i:2 * P + META * (i + 1)]).then_inc(lm_taken, 1)

            def states(c):
                dve.wait_ge(u_done, c)
                dve.wait_ge(dec_done, c)
                need(dve, o_done, c - 1)
                dve.tensor_copy(state[:, 0, :], mix[:, 2, 0:P]).then_inc(s_done, 1)
                for j in range(1, NC):
                    dve.wait_ge(s_done, NC * (c - 1) + j)
                    dve.scalar_tensor_tensor(state[:, j, :], state[:, j - 1, :], dec[:, j - 1:j],
                                             mix[:, 2, j * P:(j + 1) * P], ALU.mult, ALU.add).then_inc(s_done, 1)

            def out_scale(c):
                dve.wait_ge(rs_done, c)
                dve.wait_ge(o_copied, c)
                dve.tensor_tensor(oo[:, c - 1, :], oo[:, c - 1, :], rs[:, :], ALU.mult).then_inc(y1_done, 1)

            def gate_out(j):
                z, sg = zg[j % 3], sig_g[j % 3]
                dve.wait_ge(sig_done, 2 * HEADS + j + 1)
                col = VEC["gain_o"] + j
                dve.scalar_tensor_tensor(sg[:, :], z[:, :], vec[:, col:col + 1], sg[:, :], ALU.mult, ALU.mult).then_inc(gate_done, 1)
                dve.wait_ge(gate_done, j + 1)
                dve.wait_ge(y1_done, j + 1)
                dve.tensor_tensor(oo[:, j, :], oo[:, j, :], sg[:, :], ALU.mult).then_inc(y2_done, 1)

            def out_lo(j):
                dve.wait_ge(y_hi_done, j + 1)
                dve.tensor_tensor(y_lo[:, j, :], oo[:, j, :], y_hi[:, j, :].bitcast(F32), ALU.subtract).then_inc(y_ready, 1)

            def head(hd, m, par, gla, fin):
                def nxt(j):
                    q = 3 * par + j + 2
                    split(m + q // 2, q % 2)
                def evac(j, dst):
                    scaled_out(dst, (3 * par + j) % 2, 3 * hd + j + 1)
                if gla:
                    gla_gates(hd)
                    decays(hd)
                    dve.wait_ge(k_done, hd)
                evac(0, zf[:, :])
                if gla:
                    nxt(0)
                    level_mul(hd, 0)
                    level_mul(hd, 1)
                    qe_mul(hd)
                    ks_mul(hd)
                    level_mul(hd, 2)
                if fin:
                    out_scale(hd - 1)
                if gla:
                    level_mul(hd, 3)
                evac(1, zq[:, :])
                if gla:
                    level_mul(hd, 4)
                    level_mul(hd, 5)
                    level_one(hd)
                nxt(1)
                if gla:
                    take_level(hd, 0)
                    take_level(hd, 1)
                    states(hd)
                    take_level(hd, 2)
                    dve.wait_ge(vt_done, hd)
                evac(2, zv[:, :])
                nxt(2)
                if gla:
                    take_level(hd, 3)
                    take_level(hd, 4)
                    take_meta(hd)

            dve.wait_ge(att_zero, 2)
            dve.wait_ge(ones_set, 3)
            dve.wait_ge(mask_ready, 1)
            head(0, 0, 0, False, False)
            dve.wait_ge(lb_exp, 1)
            dve.reciprocal(tmp2_c, tmp_c).then_inc(lb_step, 1)
            dve.wait_ge(lb_step, 2)
            dve.tensor_tensor(tmp_c, tmp_c, tmp2_c, ALU.mult).then_inc(lb_step, 1)
            dve.wait_ge(lb_step, 3)
            dve.tensor_tensor(lb_c, tmp_c, tmp_c, ALU.subtract).then_inc(lb_step, 1)
            dve.wait_ge(lb_step, 4)
            dve.tensor_scalar(oml_c, lb_c, -1.0, 1.0, ALU.mult, ALU.add).then_inc(lb_step, 1)
            dve.tensor_scalar(noml_c, lb_c, 1.0, -1.0, ALU.mult, ALU.add).then_inc(lb_step, 1)
            dve.wait_ge(lam_exp, 1)
            dve.tensor_tensor(nlam, lame[:, 1:2], lame[:, 0:1], ALU.subtract).then_inc(lam_step, 1)
            dve.wait_ge(lam_step, 1)
            dve.tensor_single_scalar(nlam, nlam, -LAM_INIT, ALU.add).then_inc(lam_step, 1)
            dve.wait_ge(lb_step, 6)
            head(1, 0, 1, True, False)
            with dve.Fori(1, HEADS // 2) as i:
                head(2 * i, 3 * i, 0, True, True)
                head(2 * i + 1, 3 * i, 1, True, True)
            head(HEADS, 3 * HEADS // 2, 0, True, True)
            gate_out(0)
            gate_out(1)
            out_lo(0)
            out_lo(1)
            for j in range(3, HEADS):
                n = 3 * HEADS + j
                scaled_out(zg[j % 3][:, :], j % 2, n + 1)
                split((n + 2) // 2, n % 2)
                if j == 3:
                    gate_out(2)
                if j == 5:
                    out_scale(HEADS)
                if j > 3:
                    out_lo(j - 1)
                gate_out(j)
                if j == 3:
                    out_lo(2)
            out_lo(HEADS - 1)

            def out_phase(b0, o0, per, n, gain):
                with dve.Fori(0, KT // 2) as i:
                    for s in range(2):
                        for j in range(per):
                            q = per * s + j
                            if j == per - 1:
                                dve.wait_ge(block_done, b0 + 2 * per * i + q + 1)
                                hk = h[:, 2 * i + s, FIRST[n]:T]
                                dve.tensor_tensor(halves(hk), out_ps(s, FIRST[n]), halves(hk), ALU.add).then_inc(drained, 1)
                            split(b0 // 2 + per * i + (q + 2) // 2, q % 2)
                        norm_tile(n, 2 * i + s, gain)

            def ffn_up(b0, o0, f, n):
                cw = VEC[f"conv_w_{'ab'[f]}"]
                m0 = META * f
                dve.wait_ge(rstd_ready, n + 1)

                def tail_lo(p):
                    dve.wait_ge(act_hi_done, FT * f + p + 1)
                    dve.tensor_tensor(act_lo[:, p, m0:T], am[:, m0:T], act_hi[:, p, m0:T].bitcast(F32), ALU.subtract).then_inc(act_ready, 1)

                def pair(p, prev):
                    for j in range(2):
                        ft = 2 * p + j
                        cnt = 2 * FT * f + ft + 1
                        need(dve, base_done, cnt - 2)
                        need(dve, conv_done, cnt - 2)
                        scaled_out(ub[j][:, 2 + FIRST[n]:T + 2], j, b0 + ft + 1, t0=FIRST[n])
                        split(b0 // 2 + p + 1, j)
                        dve.wait_ge(base_done, cnt)
                        dve.scalar_tensor_tensor(cb[j][:, m0:T], ub[j][:, m0 + 1:T + 1], vec[:, bass.ds(cw + 2 * FT + ft, 1)],
                                                 cb[j][:, m0:T], ALU.mult, ALU.add).then_inc(tap_done, 1)
                        dve.wait_ge(tap_done, cnt)
                        dve.scalar_tensor_tensor(cb[j][:, m0:T], ub[j][:, m0:T], vec[:, bass.ds(cw + ft, 1)],
                                                 cb[j][:, m0:T], ALU.mult, ALU.add).then_inc(conv_done, 1)
                        if j == 0:
                            if prev:
                                tail_lo(p - 1)
                        else:
                            need(dve, act_ready, FT * f + p)
                            dve.wait_ge(silu_done, FT * f + p + 1)
                            dve.wait_ge(conv_done, cnt)
                            dve.tensor_tensor(am[:, m0:T], sa[:, m0:T], cb[1][:, m0:T], ALU.mult).then_inc(am_done, 1)

                pair(0, False)
                with dve.Fori(1, FT) as p:
                    pair(p, True)
                tail_lo(FT - 1)

            out_phase(B_OA, O_OA, 1, 1, "norm_ffn_a")
            for j in range(2):
                dve.memset(ub[j][:, 0:2], 0.0).then_inc(pad_zero, 1)
            dve.wait_ge(pad_zero, 2)
            ffn_up(B_UA, O_UA, 0, 1)
            out_phase(B_DA, O_DA, FB, 2, "kv_norm")

            def xq_part(k0, k1):
                for k in range(k0, k1):
                    dve.wait_ge(xq_hi_done, k + 1)
                    dve.scalar_tensor_tensor(xq_lo[:, k, :], h[:, k, :], vec[:, VEC["norm_mix_b"] + k:VEC["norm_mix_b"] + k + 1],
                                             xq_hi[:, k, :].bitcast(F32), ALU.mult, ALU.subtract).then_inc(xq_ready, 1)

            xq_part(0, KT // 2)
            dve.wait_ge(rstd_ready, 3)

            def soft_max(g, ti, c):
                nq, n, _ = tile_shape(ti)
                dve.wait_ge(s_up, 10 * g + 2 * ti + c + 1)
                if n <= 512:
                    dve.tensor_reduce(nmax[0:nq, c:c + 1], mix[0:nq, 2 * c, 0:n], AX_X, ALU.max, negate=True).then_inc(max_done, 1)
                else:
                    dve.tensor_reduce(nmax[0:nq, c:c + 1], mix[0:nq, 2 * c:2 * c + 2, 0:TH], mybir.AxisListType.XY, ALU.max,
                                      negate=True).then_inc(max_done, 1)

            def combine(g, ti):
                nq, n, _ = tile_shape(ti)
                cnt = 5 * g + ti + 1
                dve.wait_ge(exp_done, 2 * cnt)
                need(dve, comb_done, cnt - 1)
                dve.reciprocal(rsum[0:nq, :], esum[0:nq, :]).then_inc(rec_done, 1)
                dve.wait_ge(rec_done, 2 * cnt - 1)
                dve.tensor_tensor(nlr[0:nq, :], rsum[0:nq, 1:2], nlam[0:nq, :], ALU.mult).then_inc(rec_done, 1)
                need(dve, at_done, cnt - 1)
                dve.tensor_scalar(attn[0:nq, 0:n], prob[0][0:nq, 0:n], rsum[0:nq, 0:1], None, ALU.mult).then_inc(scaled, 1)
                dve.wait_ge(rec_done, 2 * cnt)
                dve.wait_ge(scaled, cnt)
                dve.scalar_tensor_tensor(attn[0:nq, 0:n], prob[1][0:nq, 0:n], nlr[0:nq, :], attn[0:nq, 0:n],
                                         ALU.mult, ALU.add).then_inc(comb_done, 1)

            def att_out(g, par):
                dve.wait_ge(ao_rs, g + 1)
                o = o_att[par][:, :]
                dve.scalar_tensor_tensor(o, o, sub_c, rs_att[:, :], ALU.mult, ALU.mult).then_inc(ao_y, 1)

            def att_lo(g, par):
                dve.wait_ge(y_hi_done, HEADS + g + 1)
                dve.tensor_tensor(y_lo[:, g, :], o_att[par][:, :], y_hi[:, g, :].bitcast(F32), ALU.subtract).then_inc(y_ready, 1)

            def kq_lo(hd, j, hi, lo):
                dve.wait_ge(kq_hi_done, 2 * hd + j + 1)
                dve.tensor_tensor(lo[:, :], zkq[:, :], hi[:, :].bitcast(F32), ALU.subtract).then_inc(kq_ready, 1)

            def kvq(hd, m, par, blocks_too, attend, fin):
                def nxt(j):
                    q = 3 * par + j + 2
                    split(m + q // 2, q % 2)
                g, gp, gg = hd - 1, 1 - par, hd - 2
                if attend:
                    soft_max(g, 0, 0)
                    soft_max(g, 0, 1)
                    soft_max(g, 1, 0)
                    combine(g, 0)
                    soft_max(g, 1, 1)
                    combine(g, 1)
                    if blocks_too:
                        nxt(-1)
                    soft_max(g, 2, 0)
                    soft_max(g, 2, 1)
                if blocks_too:
                    need(dve, kq_ready, 2 * hd)
                    scaled_out(zkq[:, :], 0, B_KVQ + 3 * hd + 1)
                if attend:
                    combine(g, 2)
                if blocks_too:
                    nxt(0)
                if not attend:
                    xq_part(KT // 2, KT)
                if attend:
                    soft_max(g, 3, 0)
                    soft_max(g, 3, 1)
                    if not blocks_too:
                        att_out(gg, par)
                    combine(g, 3)
                    soft_max(g, 4, 0)
                    if not blocks_too:
                        att_lo(gg, par)
                if fin and blocks_too:
                    att_out(gg, par)
                if blocks_too:
                    kq_lo(hd, 0, kh_hi[par], kh_lo[par])
                if blocks_too:
                    need(dve, va_done, hd)
                    scaled_out(zva[:, :], 0 if attend else 1, B_KVQ + 3 * hd + 2)
                if attend:
                    soft_max(g, 4, 1)
                if blocks_too:
                    nxt(1)
                if attend:
                    combine(g, 4)
                if not blocks_too:
                    nxt(-1)
                if fin and blocks_too:
                    att_lo(gg, par)
                if blocks_too:
                    dve.wait_ge(kq_ready, 2 * hd + 1)
                    scaled_out(zkq[:, :], 0, B_KVQ + 3 * hd + 3, Q_SCALE)
                    kq_lo(hd, 1, qh_hi, qh_lo)

            mb = B_KVQ // 2
            kvq(0, mb, 0, True, False, False)
            kvq(1, mb, 1, True, True, False)
            with dve.Fori(1, HEADS // 2) as i:
                kvq(2 * i, mb + 3 * i, 0, True, True, True)
                kvq(2 * i + 1, mb + 3 * i, 1, True, True, True)
            kvq(HEADS, mb + 3 * HEADS // 2, 0, False, True, True)
            att_out(HEADS - 1, 1)
            att_lo(HEADS - 1, 1)

            out_phase(B_OB, O_OB, 1, 3, "norm_ffn_b")
            ffn_up(B_UB, O_UB, 1, 3)
            for m in range(KT):
                for j in range(FB):
                    q = FB * m + j + 2
                    if j == FB - 1:
                        dve.wait_ge(block_done, B_DB + q - 1)
                        hm = halves(h[:, m, META:T])
                        dve.tensor_tensor(hm, out_ps(m % 2, META), hm, ALU.add).then_inc(drained, 1)
                    if q < FB * KT:
                        split(B_DB // 2 + q // 2, q % 2)
            dve.wait_ge(rstd_ready, 5)
            dve.wait_ge(drained, NOUTS)
            for k in range(KT):
                if k in POOL_TILES:
                    continue
                dve.scalar_tensor_tensor(h[:, k, META:T], h[:, k, META:T],
                                         vec[:, VEC["final_norm"] + k:VEC["final_norm"] + k + 1], rstd[:, META:T],
                                         ALU.mult, ALU.mult).then_inc(out_ready, 1)

        @block.tensor
        def _(pe):
            def tiles(w, s, first, last, hi, lo, ready, ks, j0=0, t0=0):
                n, w2 = len(ks), (T - t0) // 2
                for j, k in enumerate(ks):
                    if ready is not None:
                        pe.wait_ge(ready[0], ready[1] + k + 1)
                    c = slice((j0 + j) * P, (j0 + j + 1) * P)
                    for p, (wt, xt) in enumerate(((w_hi, hi), (w_hi, lo), (w_lo, hi))):
                        for a in range(2):
                            mm = pe.matmul(prod[:, s, a, 0:w2], wt[:, w, c], xt[:, k, t0 + a * w2:t0 + (a + 1) * w2],
                                           start=first and j == 0 and p == 0, stop=last and j == n - 1 and p == 2)
                return mm

            def product(m, w, o, s, hi=x_hi, lo=x_lo, ready=None, free=None, k0=0, k1=KT, t0=0):
                if k0 == 0:
                    pe.wait_ge(lo_ready, 2 * m + w + 1)
                    need(pe, drained, o - 1 if free is None else free)
                mm = tiles(w, s, k0 == 0, k1 == KT, hi, lo, ready, range(k0, k1), k0, t0)
                if k1 == KT:
                    mm.then_inc(block_done, 1)

            def norm_sum(n):
                pe.wait_ge(sq_added, KT * (n + 1) if n < 4 else KT * (n + 1) - 1)
                t0 = FIRST[n]
                w2 = (T - t0) // 2
                for a in range(2):
                    mm = pe.matmul(mix[:, a, 0:w2], ones[:, :], sqsum[:, t0 + a * w2:t0 + (a + 1) * w2], start=True,
                                   stop=n < 4)
                if n == 4:
                    pe.wait_ge(sq_done, KT * (n + 1))
                    for a in range(2):
                        mm = pe.matmul(mix[:, a, 0:w2], ones[:, :], sqb[:, 1, t0 + a * w2:t0 + (a + 1) * w2], start=False,
                                       stop=True)
                mm.then_inc(ms_done, 1)

            def v_transpose(c):
                pe.wait_ge(drained, 3 * c)
                if isinstance(c, int) and c == 1:
                    pe.wait_ge(lam_exp, 1)
                    pe.wait_ge(bf_ready, 2)
                need(pe, o_copied, c - 1)
                for j in range(NC):
                    pe.transpose(mix[:, 2, j * P:(j + 1) * P], zv[:, META + j * P:META + (j + 1) * P], ident)
                pe.transpose(mix[0:META, 3, 0:P], zv[:, 0:META], ident).then_inc(vt_done, 1)

            def k_transpose(c):
                pe.wait_ge(ks_done, c)
                pe.wait_ge(vt_copied, c)
                for j in range(NC - 1):
                    pe.transpose(mix[:, 2, j * P:(j + 1) * P], ks[:, META + j * P:META + (j + 1) * P], ident)
                pe.transpose(mix[0:META, 3, P:2 * P], ks[:, 0:META], ident).then_inc(kt_done, 1)

            def updates(c):
                pe.wait_ge(kt_copied, c)
                pe.matmul(mix[:, 2, 0:P], k_meta_t[:, :], v_meta_t[:, :], start=True, stop=True)
                for j in range(NC - 1):
                    mm = pe.matmul(mix[:, 2, (j + 1) * P:(j + 2) * P], k_t[:, j, :], v_t[:, j, :], start=True, stop=True)
                mm.then_inc(u_done, 1)

            def level64(c):
                pe.wait_ge(lev_done, 6 * (c - 1) + 1)
                need(pe, rs_done, c - 1)
                for j in range(NC):
                    a = META + j * P
                    mm = pe.matmul(mix[0:64, 0, j * 64:(j + 1) * 64], lev[:, 0, a:a + 64], lev[:, 0, a + 64:a + P],
                                   start=True, stop=True)
                mm.then_inc(lp_done, 1)

            def level32(c):
                pe.wait_ge(lev_done, 6 * (c - 1) + 2)
                for r in (0, 64):
                    for j in range(NC):
                        a = META + j * P + r
                        mm = pe.matmul(mix[r:r + 32, 1, j * 32:(j + 1) * 32], lev[:, 1, a:a + 32], lev[:, 1, a + 32:a + 64],
                                       start=True, stop=True)
                mm.then_inc(lp_done, 1)

            def level_masked(c, i):
                if i < 4:
                    pe.wait_ge(lev_done, 6 * (c - 1) + 3 + i)
                    k, q = lev[:, 2 + i, :], lev[:, 2 + i, :]
                else:
                    pe.wait_ge(one_done, c)
                    k, q = kk[:, :], qq[:, :]
                if i < 2:
                    pe.wait_ge(lp_copied, 2 * (c - 1) + 1 + i)
                else:
                    pe.wait_ge(lp_taken, 5 * (c - 1) + i - 1)
                for j in range(NC):
                    a = META + j * P
                    mm = pe.matmul(mix[:, i % 2, j * P:(j + 1) * P], k[:, a:a + P], q[:, a:a + P], start=True, stop=True)
                mm.then_inc(lp_done, 1)

            def levels_meta(c):
                for i in range(1, 5):
                    k, q = (lev[:, 2 + i, :], lev[:, 2 + i, :]) if i < 4 else (kk[:, :], qq[:, :])
                    mm = pe.matmul(mix[0:META, 3, 2 * P + META * i:2 * P + META * (i + 1)], k[:, 0:META], q[:, 0:META],
                                   start=True, stop=True)
                mm.then_inc(lm_done, 1)

            def outputs(c):
                pe.wait_ge(lp_taken, 5 * c)
                pe.wait_ge(lm_taken, 4 * c)
                pe.wait_ge(s_done, NC * c)
                pe.wait_ge(qe_done, c)
                for j in range(NC):
                    a = META + j * P
                    pe.matmul(mix[:, 2, j * P:(j + 1) * P], v_t[:, j, :], att[:, j, :], start=True, stop=False)
                    pe.matmul(mix[:, 2, j * P:(j + 1) * P], state[:, j, :], qe[:, a:a + P], start=False, stop=True)
                pe.matmul(mix[:, 3, 0:META], v_meta_t[:, :], att_meta[:, :], start=True, stop=True).then_inc(o_done, 1)

            def out_sum(c):
                pe.wait_ge(osq_done, c)
                pe.wait_ge(lp_taken, 5 * c)
                for a in range(2):
                    mm = pe.matmul(mix[:, a, 0:TH], ones[:, :], osq[:, a * TH:(a + 1) * TH], start=True, stop=True)
                mm.then_inc(os_done, 1)

            def head(hd, m, par, gla, fin):
                def blk(j, k0, k1, ready=None):
                    q = 3 * par + j
                    product(m + q // 2, q % 2, 3 * hd + j, q % 2, ready=ready, k0=k0, k1=k1)
                if not gla:
                    blk(0, 0, 5, (x_ready, 0))
                    for k in range(5, KT):
                        blk(0, k, k + 1, (x_ready, 0))
                        blk(1, k - 5, k - 4)
                    blk(1, KT - 5, KT - 3)
                    norm_sum(0)
                    blk(1, KT - 3, KT)
                    pe.wait_ge(lam_prod, 1)
                    pe.matmul(mix[:, 2, 0:2], ones[0:DH, :], lamv, start=True, stop=True).then_inc(lam_sum, 1)
                    blk(2, 0, KT)
                    return
                blk(0, 0, KT)
                blk(1, 0, 2)
                if fin:
                    outputs(hd - 1)
                blk(1, 2, 6)
                if fin:
                    out_sum(hd - 1)
                v_transpose(hd)
                blk(1, 6, KT)
                blk(2, 0, 1)
                level64(hd)
                level32(hd)
                blk(2, 1, 3)
                level_masked(hd, 0)
                k_transpose(hd)
                blk(2, 3, 4)
                level_masked(hd, 1)
                blk(2, 4, 6)
                updates(hd)
                blk(2, 6, 7)
                level_masked(hd, 2)
                blk(2, 7, KT)
                level_masked(hd, 3)
                level_masked(hd, 4)
                levels_meta(hd)

            pe.wait_ge(ones_set, 3)
            head(0, 0, 0, False, False)
            pe.wait_ge(rstd_ready, 1)
            head(1, 0, 1, True, False)
            with pe.Fori(1, HEADS // 2) as i:
                head(2 * i, 3 * i, 0, True, True)
                head(2 * i + 1, 3 * i, 1, True, True)
            head(HEADS, 3 * HEADS // 2, 0, True, True)
            for j in range(3, HEADS):
                n = 3 * HEADS + j
                product(n // 2, n % 2, n, n % 2)
                if j == 3:
                    outputs(HEADS)
                if j == 4:
                    out_sum(HEADS)

            def out_model(b0, o0, y0, n, k0, ahead):
                if k0 == 0:
                    product(b0 // 2, 0, o0, 0, y_hi, y_lo, (y_ready, y0), k1=KT - 1, t0=FIRST[n])
                product(b0 // 2, 1, o0 + 1, 1, y_hi, y_lo, (y_ready, y0), free=o0, k1=ahead, t0=FIRST[n])
                for s, k in ((0, KT - 1), (1, ahead)):
                    product(b0 // 2, s, o0 + s, s, y_hi, y_lo, (y_ready, y0), k0=k, t0=FIRST[n])
                with pe.Fori(1, KT // 2) as i:
                    for s in range(2):
                        product(b0 // 2 + i, s, o0 + 2 * i + s, s, y_hi, y_lo, (y_ready, y0), t0=FIRST[n])

            def ffn_up(b0, o0, n):
                for s in range(2):
                    product(b0 // 2, s, o0 + s, s, ready=(x_ready, KT * n) if s == 0 else None, t0=FIRST[n])
                    if s == 0:
                        norm_sum(n)
                with pe.Fori(1, FT) as p:
                    for s in range(2):
                        product(b0 // 2 + p, s, o0 + 2 * p + s, s, t0=FIRST[n])

            def ffn_down(b0, o0, f):
                with pe.Fori(0, KT // 2) as i:
                    for s in range(2):
                        for j in range(FB):
                            q = FB * s + j
                            pe.wait_ge(lo_ready, b0 + 2 * FB * i + q + 1)
                            if j == 0:
                                pe.wait_ge(drained, o0 + 2 * i + s - 1)
                            tiles(q % 2, s, j == 0, j == FB - 1, act_hi, act_lo, (act_ready, FT * f),
                                  range(KT * j, min(KT * (j + 1), FT)), t0=META * f).then_inc(block_done, 1)

            out_model(B_OA, O_OA, 0, 1, 0, 3)
            pe.wait_ge(rs_done, HEADS)
            ffn_up(B_UA, O_UA, 1)
            ffn_down(B_DA, O_DA, 0)

            def scores(g, ti, c, par):
                nq, n, q0 = tile_shape(ti)
                u = 2 * ti + c
                if u == 0:
                    pe.wait_ge(kq_ready, 2 * g + 2)
                need(pe, exp_done, 10 * g + u - 1)
                r = slice(c * DH, (c + 1) * DH)
                khi, klo = kh_hi[par], kh_lo[par]
                for bank, (a, b) in enumerate(((0, n),) if n <= 512 else ((0, TH), (TH, T))):
                    has, w = b == n, min(nq, P)

                    def bias(first):
                        return pe.matmul(mix[0:nq, 2 * c + bank, b - a - w:b - a], ident_b[:, 0:nq], causal_b[:, 0:w],
                                         start=first, stop=not first)
                    if ti == 0:
                        bias(True)
                    for p, (q, k) in enumerate(((qh_hi, khi), (qh_hi, klo), (qh_lo, khi))):
                        mm = pe.matmul(mix[0:nq, 2 * c + bank, 0:b - a], q[r, q0:q0 + nq], k[r, a:b],
                                       start=p == 0 and ti > 0, stop=p == 2 and (ti == 0 or not has))
                    if has and ti:
                        mm = bias(False)
                mm.then_inc(s_up, 1)

            def a_transpose(g, ti):
                nq, n, _ = tile_shape(ti)
                need(pe, pv_copied, 5 * g + ti)
                if ti == 0:
                    pe.wait_ge(va_copied, g + 1)
                pe.wait_ge(comb_done, 5 * g + ti + 1)
                if ti == 0:
                    pe.matmul(prod[0:META, 1, 1, 256:256 + META], ident_b[:, 0:META], ident_b[:, 0:META],
                              start=True, stop=True)
                for j in range(ti):
                    pe.transpose(prod[:, 1, 0, j * P:(j + 1) * P], attn[:, META + j * P:META + (j + 1) * P], ident)
                pe.transpose(prod[0:META, 1, 1, 0:nq], attn[0:nq, 0:META], ident[0:nq, 0:nq]).then_inc(at_done, 1)

            def attend_v(g, ti):
                nq, n, _ = tile_shape(ti)
                pe.wait_ge(at_copied, 5 * g + ti + 1)
                o = prod[:, 1, 1, P:P + nq]
                mm = pe.matmul(o, v_meta_h[:, :], attn_mt[:, 0:nq], start=True, stop=ti == 0)
                for j in range(ti):
                    mm = pe.matmul(o, v_h[:, j, :], attn_t[:, j, :], start=False, stop=j == ti - 1)
                mm.then_inc(pv_done, 1)

            def att_sum(g):
                pe.wait_ge(ao_sq, g + 1)
                pe.wait_ge(exp_done, 10 * g + 10)
                for a in range(2):
                    mm = pe.matmul(mix[:, 2 * a + 1, 0:TH], ones[:, :], osq_att[:, a * TH:(a + 1) * TH], start=True, stop=True)
                mm.then_inc(ao_sum, 1)

            def va_transpose(hd):
                pe.wait_ge(drained, O_KVQ + 3 * hd + 2)
                for j in range(NC):
                    pe.transpose(prod[:, 1, 0, j * P:(j + 1) * P], zva[:, META + j * P:META + (j + 1) * P], ident)
                need(pe, pv_copied, 5 * hd)
                pe.transpose(prod[0:META, 1, 1, 0:P], zva[:, 0:META], ident).then_inc(va_done, 1)

            def kvq(hd, m, par, attend, fin):
                def blk(j, k0, k1):
                    q = 3 * par + j
                    o = O_KVQ + 3 * hd + j
                    hi, lo = (xq_hi, xq_lo) if j == 2 else (x_hi, x_lo)
                    ready = None if attend else ((x_ready, 2 * KT), None, (xq_ready, 0))[j]
                    s = 0 if attend else j % 2
                    product(m + q // 2, q % 2, o, s, hi, lo, ready, o if attend else o - 1, k0, k1)
                g, gp = hd - 1, 1 - par
                if not attend:
                    blk(0, 0, 5)
                    norm_sum(2)
                    blk(0, 5, KT)
                    blk(1, 0, KT)
                    blk(2, 0, KT)
                    va_transpose(hd)
                    return
                blk(0, 0, 1)
                scores(g, 0, 0, gp)
                scores(g, 0, 1, gp)
                blk(0, 1, 2)
                scores(g, 1, 0, gp)
                scores(g, 1, 1, gp)
                blk(0, 2, 4)
                a_transpose(g, 0)
                blk(0, 4, 5)
                scores(g, 2, 0, gp)
                attend_v(g, 0)
                blk(0, 5, 6)
                scores(g, 2, 1, gp)
                blk(0, 6, 7)
                a_transpose(g, 1)
                blk(0, 7, KT)
                if fin:
                    att_sum(g - 1)
                scores(g, 3, 0, gp)
                attend_v(g, 1)
                blk(1, 0, 2)
                scores(g, 3, 1, gp)
                blk(1, 2, 3)
                a_transpose(g, 2)
                blk(1, 3, 4)
                scores(g, 4, 0, gp)
                attend_v(g, 2)
                blk(1, 4, KT)
                a_transpose(g, 3)
                scores(g, 4, 1, gp)
                attend_v(g, 3)
                blk(2, 0, 6)
                a_transpose(g, 4)
                blk(2, 6, KT)
                attend_v(g, 4)
                va_transpose(hd)

            def last_head(g, gp):
                def fill(k):
                    product(B_OB // 2, 0, O_OB, 0, y_hi, y_lo, (y_ready, HEADS), O_OB, k, k + 1, FIRST[3])
                fill(0)
                scores(g, 0, 0, gp)
                scores(g, 0, 1, gp)
                att_sum(g - 1)
                scores(g, 1, 0, gp)
                scores(g, 1, 1, gp)
                fill(1)
                a_transpose(g, 0)
                fill(2)
                scores(g, 2, 0, gp)
                attend_v(g, 0)
                fill(3)
                scores(g, 2, 1, gp)
                a_transpose(g, 1)
                scores(g, 3, 0, gp)
                attend_v(g, 1)
                scores(g, 3, 1, gp)
                fill(4)
                a_transpose(g, 2)
                scores(g, 4, 0, gp)
                attend_v(g, 2)
                scores(g, 4, 1, gp)
                a_transpose(g, 3)
                fill(5)
                attend_v(g, 3)
                a_transpose(g, 4)
                fill(6)
                attend_v(g, 4)
                att_sum(g)

            mb = B_KVQ // 2
            kvq(0, mb, 0, False, False)
            pe.wait_ge(rstd_ready, 3)
            kvq(1, mb, 1, True, False)
            with pe.Fori(1, HEADS // 2) as i:
                kvq(2 * i, mb + 3 * i, 0, True, True)
                kvq(2 * i + 1, mb + 3 * i, 1, True, True)
            last_head(HEADS - 1, 1)
            out_model(B_OB, O_OB, HEADS, 3, KT - 1, 6)
            pe.wait_ge(ao_rs, HEADS)
            ffn_up(B_UB, O_UB, 3)
            ffn_down(B_DB, O_DB, 1)
            norm_sum(4)


def tile_shape(ti):
    return (META, META, 0) if ti == 0 else (P, META + P * ti, META + P * (ti - 1))


def kernel(**inputs):
    import numpy as np
    import concourse.bacc as bacc
    from concourse.bass_utils import run_bass_kernel_spmd

    a = {k: np.asarray(v) for k, v in inputs.items()}

    def tiles_of(w):
        k, m = w.shape
        return w.reshape(k // P, P, m // P, P).transpose(2, 1, 0, 3).reshape(m // P, P, k)

    def in_blocks(w):
        t = tiles_of(w)
        t = np.concatenate([t, np.zeros((t.shape[0], P, FB * KT * P - t.shape[2]), np.float32)], axis=2)
        return t.reshape(-1, P, FB, KT * P).transpose(0, 2, 1, 3).reshape(-1, P, KT * P)

    w_in = tiles_of(a["hg_w_in"][0]).reshape(4, HEADS, P, D)
    w_kv = tiles_of(a["w_kv"]).reshape(2, HEADS, P, D)
    w_q = tiles_of(a["da_w_q"][0])

    def up(l):
        return tiles_of(a["ffn_w_up"][l]).reshape(2, FT, P, D).transpose(1, 0, 2, 3).reshape(2 * FT, P, D)

    wstream = np.concatenate([
        w_in[[1, 0, 2]].transpose(1, 0, 2, 3).reshape(3 * HEADS, P, D), w_in[3],
        tiles_of(a["hg_w_o"][0]), up(0), in_blocks(a["ffn_w_down"][0]),
        np.stack([w_kv[0], w_kv[1], w_q], axis=1).reshape(3 * HEADS, P, D),
        tiles_of(a["da_w_o"][0]), up(1), in_blocks(a["ffn_w_down"][1])])

    def cols(v):
        return v.reshape(-1, P).T

    def pairs(v):
        return cols(v.reshape(2, FT, P).transpose(1, 0, 2).reshape(-1))

    lam = np.stack([a[n][0] for n in ("da_lam_q1", "da_lam_q2", "da_lam_k1", "da_lam_k2")], axis=1)
    lam = np.concatenate([lam, np.zeros((P - DH, 4), np.float32)])
    vecs = np.concatenate(
        [cols(a["norm_mix"][0]), cols(a["norm_mix"][1]), cols(a["norm_ffn"][0]), cols(a["norm_ffn"][1]),
         cols(a["hg_lb"][0]), cols(a["hg_gain_o"][0]), cols(a["kv_norm"]), cols(a["final_norm"]),
         cols(a["da_sub_gain"][0]), lam]
        + [pairs(a["ffn_conv_w"][l, t]) for l in range(2) for t in range(3)]
        + [pairs(a["ffn_conv_b"][l]) for l in range(2)], axis=1)

    i = np.arange(P)
    keep = np.ones((P, T), np.float32)
    keep[:, 0] = 0
    keep[:, META::P] = 0
    s, t = i[:, None], i[None, :]
    masks = np.stack([(s // (2 * w) == t // (2 * w)) & ((s % (2 * w) < w) & (t % (2 * w) >= w) if w > 1 else s <= t)
                      for w in MASKED_LEVELS], axis=1).astype(np.float32)
    consts = np.concatenate([np.eye(P, dtype=np.float32),
                             np.where(i[None, :] > i[:, None], np.float32(MASKED), np.float32(0)), keep,
                             masks.reshape(P, -1)], axis=1)

    arrays = {
        "wstream": wstream,
        "xT": np.ascontiguousarray(a["x"][0].T.reshape(KT, P, SEQ).transpose(1, 0, 2)),
        "metaT": np.ascontiguousarray(a["meta_tokens"].T.reshape(KT, P, META).transpose(1, 0, 2)),
        "vecs": np.ascontiguousarray(vecs), "consts": np.ascontiguousarray(consts)}
    nc = bacc.Bacc("TRN2", target_bir_lowering=False, num_devices=1)
    aps = [nc.dram_tensor(n, v.shape, mybir.dt.from_np(v.dtype), kind="ExternalInput").ap() for n, v in arrays.items()]
    result = nc.dram_tensor("result", (KT, P, SEQ), F32, kind="ExternalOutput").ap()
    build(nc, *aps, result)
    r = run_bass_kernel_spmd(nc, [arrays], core_ids=[0])
    return r.results[0]["result"].reshape(D, SEQ).T.reshape(1, SEQ, D)
```
